# Optimizing a Trainium2 kernel written in Bass

```python
import math
import jax, jax.numpy as jnp
from jax import lax
import numpy as np

D_MODEL = 1024
BATCH = 1
SEQ = 512
DEPTH = 2

N_A_LAYERS = DEPTH // 2
N_B_LAYERS = DEPTH - N_A_LAYERS
D_FF = 4 * D_MODEL
NORM_EPS = 1e-6
NEG = -1e30

DIFF_HEAD_DIM = 64
DIFF_HEADS = D_MODEL // (2 * DIFF_HEAD_DIM)
Q_BLOCK = 128

REL_BUCKETS = 32
REL_MAX_DIST = 128
REL_HEADS = 2 * DIFF_HEADS

NSA_HEAD_DIM = 64
NSA_HEADS = D_MODEL // NSA_HEAD_DIM
NSA_KV_HEADS = 4
NSA_GROUP = NSA_HEADS // NSA_KV_HEADS
CMP_LEN = 32
CMP_STRIDE = 16
CMP_HIDDEN = 256
SLC_LEN = 64
SLC_TOPK = 16
SLC_FORCED_LOCAL = 2
FORCE_BONUS = 1e4
WINDOW = 512
NSA_Q_BLOCK = 32
NSA_IN_COLS = NSA_HEADS * NSA_HEAD_DIM + 3 * NSA_HEADS
KV_COLS = 6 * NSA_KV_HEADS * NSA_HEAD_DIM


def rms_norm(x, g):
    xf = x.astype(jnp.float32)
    y = xf * lax.rsqrt(jnp.mean(xf * xf, axis=-1, keepdims=True) + NORM_EPS)
    return (y * g.astype(jnp.float32)).astype(x.dtype)

def modulate(h, shift, scale):
    return h * (1 + scale) + shift

def t5_bucket(dist):
    n = jnp.maximum(dist, 0)
    max_exact = REL_BUCKETS // 2
    nf = jnp.maximum(n, 1).astype(jnp.float32)
    large = max_exact + (jnp.log(nf / max_exact) / math.log(REL_MAX_DIST / max_exact)
                         * (REL_BUCKETS - max_exact)).astype(jnp.int32)
    large = jnp.minimum(large, REL_BUCKETS - 1)
    return jnp.where(n < max_exact, n, large)

def squared_relu_mlp(h, w1, w2):
    return jnp.square(jax.nn.relu(h @ w1)) @ w2

def diff_attention(h, w_in, w_out, lam, subln, rel_bias, layer_idx):
    B, T, _ = h.shape
    H, d = DIFF_HEADS, DIFF_HEAD_DIM
    q, k, v = jnp.split(h @ w_in, 3, axis=-1)
    q = q.reshape(B, T, H, 2, d)
    k = k.reshape(B, T, H, 2, d)
    v = v.reshape(B, T, H, 2 * d)
    lam_init = 0.8 - 0.6 * math.exp(-0.3 * layer_idx)
    lf = lam.astype(jnp.float32)
    lam_full = jnp.exp(jnp.sum(lf[0] * lf[1])) - jnp.exp(jnp.sum(lf[2] * lf[3])) + lam_init
    bias_tab = rel_bias.reshape(REL_BUCKETS, H, 2).astype(jnp.float32)
    k_pos = jnp.arange(T)
    scale = d ** -0.5
    nblk = T // Q_BLOCK
    qb = q.reshape(B, nblk, Q_BLOCK, H, 2, d).transpose(1, 0, 2, 3, 4, 5)

    def block(args):
        qi, blk = args
        q_pos = blk * Q_BLOCK + jnp.arange(Q_BLOCK)
        dist = q_pos[:, None] - k_pos[None, :]
        bias = bias_tab[t5_bucket(dist)].transpose(2, 3, 0, 1)
        s = jnp.einsum('bqhmd,bkhmd->bhmqk', qi, k,
                       preferred_element_type=jnp.float32) * scale + bias[None]
        s = jnp.where((dist >= 0)[None, None, None], s, NEG)
        p = jax.nn.softmax(s, axis=-1)
        a = p[:, :, 0] - lam_full * p[:, :, 1]
        return jnp.einsum('bhqk,bkhe->bqhe', a.astype(v.dtype), v)

    o = lax.map(block, (qb, jnp.arange(nblk)))
    o = o.transpose(1, 0, 2, 3, 4).reshape(B, T, H, 2 * d)
    o = rms_norm(o, subln) * (1 - lam_init)
    return o.reshape(B, T, H * 2 * d) @ w_out

def nsa_shared_kv(h, w_kv, cmp_pos, cmp_w1, cmp_w2):
    B, T, _ = h.shape
    G, d = NSA_KV_HEADS, NSA_HEAD_DIM
    kv = (h @ w_kv).reshape(B, T, 6, G, d).transpose(2, 0, 3, 1, 4)
    n_cmp = (T - CMP_LEN) // CMP_STRIDE + 1
    idx = jnp.arange(n_cmp)[:, None] * CMP_STRIDE + jnp.arange(CMP_LEN)[None, :]
    blocks = kv[0:2][:, :, :, idx] + cmp_pos[:, None, None, None]
    flat = blocks.reshape(2, B, G, n_cmp, CMP_LEN * d)
    hid = jax.nn.gelu(jnp.einsum('sbgnf,sfh->sbgnh', flat, cmp_w1))
    cmp = jnp.einsum('sbgnh,shd->sbgnd', hid, cmp_w2)
    return (cmp[0], cmp[1], kv[2], kv[3], kv[4], kv[5])

def nsa_attention(h, w_in, w_out, rel_bias, k_cmp, v_cmp, k_slc, v_slc, k_win, v_win):
    B, T, _ = h.shape
    H, G, R, d = NSA_HEADS, NSA_KV_HEADS, NSA_GROUP, NSA_HEAD_DIM
    proj = h @ w_in
    q = proj[..., :H * d].reshape(B, T, G, R, d)
    gates = jax.nn.sigmoid(proj[..., H * d:].astype(jnp.float32)).reshape(B, T, G, R, 3)
    scale = d ** -0.5
    bias_tab = rel_bias.reshape(REL_BUCKETS, G, R).astype(jnp.float32)
    bias_tab_g = bias_tab.transpose(1, 0, 2)
    n_cmp = k_cmp.shape[2]
    n_slc = T // SLC_LEN
    top_k = min(SLC_TOPK, n_slc)
    cmp_start = jnp.arange(n_cmp) * CMP_STRIDE
    cmp_end = cmp_start + CMP_LEN - 1
    slc_start = jnp.arange(n_slc) * SLC_LEN
    overlap = ((cmp_start[:, None] < slc_start[None, :] + SLC_LEN)
               & (cmp_end[:, None] >= slc_start[None, :])).astype(jnp.float32)
    k_slc_blk = k_slc.reshape(B, G, n_slc, SLC_LEN, d)
    v_slc_blk = v_slc.reshape(B, G, n_slc, SLC_LEN, d)
    k_win_pad = jnp.pad(k_win, ((0, 0), (0, 0), (WINDOW, 0), (0, 0)))
    v_win_pad = jnp.pad(v_win, ((0, 0), (0, 0), (WINDOW, 0), (0, 0)))
    b_idx = jnp.arange(B)[:, None, None, None]
    g_idx = jnp.arange(G)[None, :, None, None]
    j_idx = jnp.arange(n_slc)
    in_offs = jnp.arange(SLC_LEN)
    nblk = T // NSA_Q_BLOCK
    qb = q.reshape(B, nblk, NSA_Q_BLOCK, G, R, d).transpose(1, 0, 2, 3, 4, 5)
    gb = gates.reshape(B, nblk, NSA_Q_BLOCK, G, R, 3).transpose(1, 0, 2, 3, 4, 5)

    def block(args):
        qi, gi, blk = args
        q_pos = blk * NSA_Q_BLOCK + jnp.arange(NSA_Q_BLOCK)
        s_c = jnp.einsum('bqgrd,bgnd->bgrqn', qi, k_cmp,
                         preferred_element_type=jnp.float32) * scale
        valid_c = cmp_end[None, :] <= q_pos[:, None]
        p_c = jax.nn.softmax(jnp.where(valid_c, s_c, NEG), axis=-1) * valid_c
        o_c = jnp.einsum('bgrqn,bgnd->bqgrd', p_c.astype(v_cmp.dtype), v_cmp)
        imp = jnp.einsum('bgrqn,nj->bgqj', p_c, overlap)
        q_blk = q_pos // SLC_LEN
        forced = (j_idx[None, :] == 0) | ((j_idx[None, :] <= q_blk[:, None])
                                          & (j_idx[None, :] > q_blk[:, None] - SLC_FORCED_LOCAL))
        imp = jnp.where(forced[None, None], FORCE_BONUS, imp)
        imp = jnp.where((j_idx[None, :] <= q_blk[:, None])[None, None], imp, NEG)
        _, sel = lax.top_k(imp, top_k)
        ks = k_slc_blk[b_idx, g_idx, sel].reshape(B, G, NSA_Q_BLOCK, top_k * SLC_LEN, d)
        vs = v_slc_blk[b_idx, g_idx, sel].reshape(B, G, NSA_Q_BLOCK, top_k * SLC_LEN, d)
        pos_s = (sel[..., None] * SLC_LEN + in_offs).reshape(B, G, NSA_Q_BLOCK, top_k * SLC_LEN)
        dist_s = q_pos[None, None, :, None] - pos_s
        bias_s = bias_tab_g[g_idx, t5_bucket(dist_s)].transpose(0, 1, 4, 2, 3)
        s_s = jnp.einsum('bqgrd,bgqkd->bgrqk', qi, ks,
                         preferred_element_type=jnp.float32) * scale + bias_s
        s_s = jnp.where((dist_s >= 0)[:, :, None], s_s, NEG)
        p_s = jax.nn.softmax(s_s, axis=-1)
        o_s = jnp.einsum('bgrqk,bgqkd->bqgrd', p_s.astype(vs.dtype), vs)
        start = blk * NSA_Q_BLOCK
        kw = lax.dynamic_slice_in_dim(k_win_pad, start, WINDOW + NSA_Q_BLOCK, axis=2)
        vw = lax.dynamic_slice_in_dim(v_win_pad, start, WINDOW + NSA_Q_BLOCK, axis=2)
        k_pos = start - WINDOW + jnp.arange(WINDOW + NSA_Q_BLOCK)
        dist_w = q_pos[:, None] - k_pos[None, :]
        valid_w = (dist_w >= 0) & (dist_w < WINDOW) & (k_pos[None, :] >= 0)
        bias_w = bias_tab[t5_bucket(dist_w)].transpose(2, 3, 0, 1)
        s_w = jnp.einsum('bqgrd,bgkd->bgrqk', qi, kw,
                         preferred_element_type=jnp.float32) * scale + bias_w[None]
        p_w = jax.nn.softmax(jnp.where(valid_w[None, None, None], s_w, NEG), axis=-1)
        o_w = jnp.einsum('bgrqk,bgkd->bqgrd', p_w.astype(vw.dtype), vw)
        o = gi[..., 0:1] * o_c + gi[..., 1:2] * o_s + gi[..., 2:3] * o_w
        return o.astype(qi.dtype)

    o = lax.map(block, (qb, gb, jnp.arange(nblk)))
    o = o.transpose(1, 0, 2, 3, 4, 5).reshape(B, T, H * d)
    return o @ w_out

def first_inputs(seed: int = 0) -> dict:
    key = jax.random.key(seed)
    ks = jax.random.split(key, 24)
    f32 = jnp.float32
    D, d_a, d_n = D_MODEL, DIFF_HEAD_DIM, NSA_HEAD_DIM
    nrm = lambda k, shape, s: jax.random.normal(k, shape, f32) * s
    gain = lambda k, shape: 1.0 + 0.02 * jax.random.normal(k, shape, f32)
    return {
        "x": nrm(ks[0], (BATCH, SEQ, D), 1.0),
        "c": nrm(ks[1], (BATCH, D), 1.0),
        "rel_bias": nrm(ks[2], (REL_BUCKETS, REL_HEADS), 0.5),
        "ada_w": nrm(ks[3], (DEPTH, D, 6 * D), D ** -0.5),
        "ada_b": nrm(ks[4], (DEPTH, 6 * D), 0.02),
        "attn_norm": gain(ks[5], (DEPTH, D)),
        "mlp_norm": gain(ks[6], (DEPTH, D)),
        "mlp_w1": nrm(ks[7], (DEPTH, D, D_FF), D ** -0.5),
        "mlp_w2": nrm(ks[8], (DEPTH, D_FF, D), D_FF ** -0.5),
        "a_w_in": nrm(ks[9], (N_A_LAYERS, D, 3 * D), D ** -0.5),
        "a_w_out": nrm(ks[10], (N_A_LAYERS, D, D), D ** -0.5),
        "a_lambda": nrm(ks[11], (N_A_LAYERS, 4, d_a), 0.1),
        "a_subln": gain(ks[12], (N_A_LAYERS, 2 * d_a)),
        "kv_ada_w": nrm(ks[13], (D, 2 * D), D ** -0.5),
        "kv_ada_b": nrm(ks[14], (2 * D,), 0.02),
        "kv_norm": gain(ks[15], (D,)),
        "w_kv": nrm(ks[16], (D, KV_COLS), D ** -0.5),
        "cmp_pos": nrm(ks[17], (2, CMP_LEN, d_n), 0.1),
        "cmp_w1": nrm(ks[18], (2, CMP_LEN * d_n, CMP_HIDDEN), (CMP_LEN * d_n) ** -0.5),
        "cmp_w2": nrm(ks[19], (2, CMP_HIDDEN, d_n), CMP_HIDDEN ** -0.5),
        "b_w_in": nrm(ks[20], (N_B_LAYERS, D, NSA_IN_COLS), D ** -0.5),
        "b_w_out": nrm(ks[21], (N_B_LAYERS, D, D), D ** -0.5),
        "final_norm": gain(ks[22], (D,)),
    }

def first_block(x, c, rel_bias, ada_w, ada_b, attn_norm, mlp_norm, mlp_w1, mlp_w2,
              a_w_in, a_w_out, a_lambda, a_subln, kv_ada_w, kv_ada_b, kv_norm, w_kv,
              cmp_pos, cmp_w1, cmp_w2, b_w_in, b_w_out, final_norm):
    c_act = jax.nn.silu(c)
    shared = None
    for layer in range(DEPTH):
        mod = (c_act @ ada_w[layer] + ada_b[layer])[:, None, :]
        sh_a, sc_a, gt_a, sh_m, sc_m, gt_m = jnp.split(mod, 6, axis=-1)
        h = modulate(rms_norm(x, attn_norm[layer]), sh_a, sc_a)
        if layer < N_A_LAYERS:
            mix = diff_attention(h, a_w_in[layer], a_w_out[layer], a_lambda[layer],
                                 a_subln[layer], rel_bias, layer)
        else:
            i = layer - N_A_LAYERS
            mix = nsa_attention(h, b_w_in[i], b_w_out[i], rel_bias, *shared)
        x = x + gt_a * mix
        h = modulate(rms_norm(x, mlp_norm[layer]), sh_m, sc_m)
        x = x + gt_m * squared_relu_mlp(h, mlp_w1[layer], mlp_w2[layer])
        if layer == N_A_LAYERS - 1:
            kv_mod = (c_act @ kv_ada_w + kv_ada_b)[:, None, :]
            sh_kv, sc_kv = jnp.split(kv_mod, 2, axis=-1)
            h_kv = modulate(rms_norm(x, kv_norm), sh_kv, sc_kv)
            shared = nsa_shared_kv(h_kv, w_kv, cmp_pos, cmp_w1, cmp_w2)
    return rms_norm(x, final_norm)


N_A = DEPTH // 2
N_B = DEPTH - N_A
PLE_DIM = 256
EPS = 1e-6
ROPE_THETA = 10000.0

A_HEADS = 4
A_DQK = 128
A_DV = 256
A_QK = A_HEADS * A_DQK
A_VW = A_HEADS * A_DV
A_CONV = 4
A_CHUNK = 64
A_COLS = 2 * A_QK + 3 * A_VW + 2 * A_HEADS

B_KV_HEADS = 4
B_HD = 128
DILATED_GROUPS = ((128, 1), (512, 4), (2048, 16))
B_GROUPS = len(DILATED_GROUPS)
B_QW = B_GROUPS * B_KV_HEADS * B_HD
B_VW = B_KV_HEADS * B_HD
B_COLS = B_QW + B_VW


def rms_norm_2(x, g):
    xf = x.astype(jnp.float32)
    y = xf * lax.rsqrt(jnp.mean(xf * xf, axis=-1, keepdims=True) + EPS)
    return (y * g.astype(jnp.float32)).astype(x.dtype)

def rope_tables(seq, dim):
    inv = ROPE_THETA ** (-jnp.arange(0, dim, 2, dtype=jnp.float32) / dim)
    ang = jnp.arange(seq, dtype=jnp.float32)[:, None] * inv[None, :]
    return jnp.cos(ang), jnp.sin(ang)

def apply_rope(x, cos, sin):
    shape = (1, cos.shape[0]) + (1,) * (x.ndim - 3) + (cos.shape[1],)
    c = cos.reshape(shape)
    s = sin.reshape(shape)
    x1, x2 = jnp.split(x, 2, axis=-1)
    return jnp.concatenate([x1 * c - x2 * s, x2 * c + x1 * s], axis=-1)

def causal_depthwise_conv(x, w):
    K = w.shape[0]
    S = x.shape[1]
    xp = jnp.pad(x, ((0, 0), (K - 1, 0), (0, 0)))
    out = xp[:, 0:S] * w[0]
    for j in range(1, K):
        out = out + xp[:, j:j + S] * w[j]
    return out

def mlstm_chunkwise(q, k, v, i_pre, logf):
    Bsz, S, H, dk = q.shape
    dv = v.shape[-1]
    L = A_CHUNK
    nc = S // L

    def to_chunks(t):
        t = t.reshape((Bsz, nc, L, H) + t.shape[3:])
        return jnp.moveaxis(t, (1, 3), (0, 2))

    causal = jnp.tril(jnp.ones((L, L), dtype=bool))

    def step(carry, inp):
        C, n, m = carry
        qc, kc, vc, ic, fc = inp
        b = jnp.cumsum(fc, axis=-1)
        D = b[..., :, None] - b[..., None, :] + ic[..., None, :]
        D = jnp.where(causal, D, -jnp.inf)
        m_inter = b + m[..., None]
        m_s = jnp.maximum(m_inter, D.max(axis=-1))
        wts = jnp.exp(D - m_s[..., None]) * jnp.einsum('bhsd,bhjd->bhsj', qc, kc)
        inter = jnp.exp(m_inter - m_s)
        num = wts @ vc + inter[..., None] * jnp.einsum('bhsd,bhvd->bhsv', qc, C)
        den = wts.sum(axis=-1) + inter * jnp.einsum('bhsd,bhd->bhs', qc, n)
        h = num / jnp.maximum(jnp.abs(den), jnp.exp(-m_s))[..., None]
        g = b[..., -1:] - b + ic
        m_new = jnp.maximum(b[..., -1] + m, g.max(axis=-1))
        decay = jnp.exp(b[..., -1] + m - m_new)
        wj = jnp.exp(g - m_new[..., None])
        C = decay[..., None, None] * C + jnp.einsum('bhj,bhjv,bhjd->bhvd', wj, vc, kc)
        n = decay[..., None] * n + jnp.einsum('bhj,bhjd->bhd', wj, kc)
        return (C, n, m_new), h

    init = (jnp.zeros((Bsz, H, dv, dk), jnp.float32),
            jnp.zeros((Bsz, H, dk), jnp.float32),
            jnp.zeros((Bsz, H), jnp.float32))
    _, hs = lax.scan(step, init, (to_chunks(q), to_chunks(k), to_chunks(v),
                                  to_chunks(i_pre), to_chunks(logf)))
    return jnp.moveaxis(hs, (0, 2), (1, 3)).reshape(Bsz, S, H, dv)

def mlstm_layer(h, norm_g, w_in, conv_w, b_gate, hnorm_g, w_out):
    Bsz, S, _ = h.shape
    proj = rms_norm_2(h, norm_g) @ w_in
    qk, v, o, z, gates = jnp.split(
        proj, [2 * A_QK, 2 * A_QK + A_VW, 2 * A_QK + 2 * A_VW, 2 * A_QK + 3 * A_VW], axis=-1)
    qk = jax.nn.silu(causal_depthwise_conv(qk, conv_w)).astype(jnp.float32)
    q, k = jnp.split(qk, 2, axis=-1)
    q = q.reshape(Bsz, S, A_HEADS, A_DQK)
    k = k.reshape(Bsz, S, A_HEADS, A_DQK) * (A_DQK ** -0.5)
    v = v.astype(jnp.float32).reshape(Bsz, S, A_HEADS, A_DV)
    gates = gates.astype(jnp.float32) + b_gate.astype(jnp.float32)
    i_pre, f_pre = jnp.split(gates, 2, axis=-1)
    ht = mlstm_chunkwise(q, k, v, i_pre, jax.nn.log_sigmoid(f_pre))
    ht = jax.nn.sigmoid(o.astype(jnp.float32)).reshape(Bsz, S, A_HEADS, A_DV) * ht
    ht = rms_norm_2(ht, hnorm_g.reshape(A_HEADS, A_DV))
    y = ht.reshape(Bsz, S, A_VW) * jax.nn.silu(z.astype(jnp.float32))
    return y.astype(h.dtype) @ w_out

def dilated_window_attention(q, k, v, window, dilation):
    Bsz, S, H, hd = q.shape
    r = dilation
    n_back = window // dilation
    s_sub = S // r
    nb = -(-s_sub // Q_BLOCK)
    P = nb * Q_BLOCK

    def to_blocks(t):
        t = t.reshape(Bsz, s_sub, r, H, hd).transpose(0, 2, 3, 1, 4)
        t = jnp.pad(t, ((0, 0), (0, 0), (0, 0), (0, P - s_sub), (0, 0)))
        return t.reshape(Bsz, r, H, nb, Q_BLOCK, hd)

    def with_prev(t):
        prev = jnp.pad(t, ((0, 0), (0, 0), (0, 0), (1, 0), (0, 0), (0, 0)))[:, :, :, :-1]
        return jnp.concatenate([prev, t], axis=4)

    qb = to_blocks(q)
    kw = with_prev(to_blocks(k))
    vw = with_prev(to_blocks(v))
    s = jnp.einsum('brhnqd,brhnkd->brhnqk', qb, kw) * (hd ** -0.5)
    blk = jnp.arange(nb)[:, None, None]
    qi = jnp.arange(Q_BLOCK)[None, :, None]
    kj = jnp.arange(2 * Q_BLOCK)[None, None, :]
    dist = Q_BLOCK + qi - kj
    kpos = (blk - 1) * Q_BLOCK + kj
    mask = (dist >= 0) & (dist <= n_back) & (kpos >= 0)
    s = jnp.where(mask, s, -jnp.inf)
    mx = s.max(axis=-1, keepdims=True)
    e = jnp.exp(s - mx)
    den = e.sum(axis=-1)
    o = jnp.einsum('brhnqk,brhnkd->brhnqd', e, vw) / den[..., None]
    lse = mx[..., 0] + jnp.log(den)
    o = o.reshape(Bsz, r, H, P, hd)[:, :, :, :s_sub].transpose(0, 3, 1, 2, 4).reshape(Bsz, S, H, hd)
    lse = lse.reshape(Bsz, r, H, P)[..., :s_sub].transpose(0, 3, 1, 2).reshape(Bsz, S, H)
    return o, lse

def shared_kv(h, norm_g, w_kv, knorm_g, cos, sin):
    Bsz, S, _ = h.shape
    kv = (rms_norm_2(h, norm_g) @ w_kv).astype(jnp.float32)
    k, v = jnp.split(kv, 2, axis=-1)
    k = k.reshape(Bsz, S, B_KV_HEADS, B_HD)
    v = v.reshape(Bsz, S, B_KV_HEADS, B_HD)
    k = apply_rope(rms_norm_2(k, knorm_g), cos, sin)
    return k, v

def dilated_layer(h, k, v, norm_g, w_in, qnorm_g, w_out, cos, sin):
    Bsz, S, _ = h.shape
    proj = rms_norm_2(h, norm_g) @ w_in
    q, z = jnp.split(proj, [B_QW], axis=-1)
    q = q.astype(jnp.float32).reshape(Bsz, S, B_GROUPS, B_KV_HEADS, B_HD)
    q = apply_rope(rms_norm_2(q, qnorm_g), cos, sin)
    outs, lses = [], []
    for g, (window, dilation) in enumerate(DILATED_GROUPS):
        o_g, l_g = dilated_window_attention(q[:, :, g], k, v, window, dilation)
        outs.append(o_g)
        lses.append(l_g)
    wts = jax.nn.softmax(jnp.stack(lses, axis=0), axis=0)
    o = jnp.einsum('gbsh,gbshd->bshd', wts, jnp.stack(outs, axis=0))
    y = o.reshape(Bsz, S, B_VW) * jax.nn.silu(z.astype(jnp.float32))
    return y.astype(h.dtype) @ w_out

def ple_add(h, p_l, norm_g, w_gate, w_proj):
    gate = jax.nn.sigmoid((rms_norm_2(h, norm_g) @ w_gate).astype(jnp.float32))
    return h + ((p_l @ w_proj).astype(jnp.float32) * gate).astype(h.dtype)

def second_inputs(seed: int = 0) -> dict:
    key = jax.random.key(seed)
    ks = jax.random.split(key, 24)
    nrm = jax.random.normal
    f32 = jnp.float32
    x = nrm(ks[0], (BATCH, SEQ, D_MODEL), f32)
    p = nrm(ks[1], (DEPTH, BATCH, SEQ, PLE_DIM), f32)
    norm_a = 1.0 + 0.05 * nrm(ks[2], (N_A, D_MODEL), f32)
    w_in_a = nrm(ks[3], (N_A, D_MODEL, A_COLS), f32) * D_MODEL ** -0.5
    conv_a = nrm(ks[4], (N_A, A_CONV, 2 * A_QK), f32) * A_CONV ** -0.5
    b_i = 0.1 * nrm(ks[5], (N_A, A_HEADS), f32)
    b_f = jnp.linspace(3.0, 6.0, A_HEADS, dtype=f32)[None, :] + 0.1 * nrm(ks[6], (N_A, A_HEADS), f32)
    b_gate_a = jnp.concatenate([b_i, b_f], axis=-1)
    hnorm_a = 1.0 + 0.05 * nrm(ks[7], (N_A, A_VW), f32)
    w_out_a = nrm(ks[8], (N_A, A_VW, D_MODEL), f32) * A_VW ** -0.5
    norm_kv = 1.0 + 0.05 * nrm(ks[9], (D_MODEL,), f32)
    w_kv = nrm(ks[10], (D_MODEL, 2 * B_VW), f32) * D_MODEL ** -0.5
    knorm = 1.0 + 0.05 * nrm(ks[11], (B_HD,), f32)
    norm_b = 1.0 + 0.05 * nrm(ks[12], (N_B, D_MODEL), f32)
    w_in_b = nrm(ks[13], (N_B, D_MODEL, B_COLS), f32) * D_MODEL ** -0.5
    qnorm_b = 1.0 + 0.05 * nrm(ks[14], (N_B, B_HD), f32)
    w_out_b = nrm(ks[15], (N_B, B_VW, D_MODEL), f32) * B_VW ** -0.5
    ple_norm = 1.0 + 0.05 * nrm(ks[16], (DEPTH, D_MODEL), f32)
    w_ple_gate = nrm(ks[17], (DEPTH, D_MODEL, D_MODEL), f32) * D_MODEL ** -0.5
    w_ple = nrm(ks[18], (DEPTH, PLE_DIM, D_MODEL), f32) * PLE_DIM ** -0.5
    return {"x": x, "p": p, "norm_a": norm_a, "w_in_a": w_in_a, "conv_a": conv_a,
            "b_gate_a": b_gate_a, "hnorm_a": hnorm_a, "w_out_a": w_out_a,
            "norm_kv": norm_kv, "w_kv": w_kv, "knorm": knorm,
            "norm_b": norm_b, "w_in_b": w_in_b, "qnorm_b": qnorm_b, "w_out_b": w_out_b,
            "ple_norm": ple_norm, "w_ple_gate": w_ple_gate, "w_ple": w_ple}

def second_block(x, p, norm_a, w_in_a, conv_a, b_gate_a, hnorm_a, w_out_a,
              norm_kv, w_kv, knorm, norm_b, w_in_b, qnorm_b, w_out_b,
              ple_norm, w_ple_gate, w_ple):
    S = x.shape[1]
    cos, sin = rope_tables(S, B_HD)
    h = x
    k_sh = None
    v_sh = None
    for layer in range(DEPTH):
        if layer < N_A:
            h = h + mlstm_layer(h, norm_a[layer], w_in_a[layer], conv_a[layer],
                                b_gate_a[layer], hnorm_a[layer], w_out_a[layer])
        else:
            if layer == N_A:
                k_sh, v_sh = shared_kv(h, norm_kv, w_kv, knorm, cos, sin)
            j = layer - N_A
            h = h + dilated_layer(h, k_sh, v_sh, norm_b[j], w_in_b[j], qnorm_b[j],
                                  w_out_b[j], cos, sin)
        h = ple_add(h, p[layer], ple_norm[layer], w_ple_gate[layer], w_ple[layer])
    return h


def setup_inputs(seed=0):
    out = dict(first_inputs(seed))
    for name, value in second_inputs(seed + 1).items():
        if name != "x":
            out[name + "_2"] = value
    return out


def reference(
    x, c, rel_bias, ada_w, ada_b, attn_norm, mlp_norm, mlp_w1, mlp_w2, a_w_in, a_w_out,
    a_lambda, a_subln, kv_ada_w, kv_ada_b, kv_norm, w_kv, cmp_pos, cmp_w1, cmp_w2, b_w_in,
    b_w_out, final_norm, p_2, norm_a_2, w_in_a_2, conv_a_2, b_gate_a_2, hnorm_a_2, w_out_a_2,
    norm_kv_2, w_kv_2, knorm_2, norm_b_2, w_in_b_2, qnorm_b_2, w_out_b_2, ple_norm_2,
    w_ple_gate_2, w_ple_2,
):
    x = first_block(
        x, c, rel_bias, ada_w, ada_b, attn_norm, mlp_norm, mlp_w1, mlp_w2, a_w_in, a_w_out,
        a_lambda, a_subln, kv_ada_w, kv_ada_b, kv_norm, w_kv, cmp_pos, cmp_w1, cmp_w2, b_w_in,
        b_w_out, final_norm,
    )
    return second_block(
        x, p_2, norm_a_2, w_in_a_2, conv_a_2, b_gate_a_2, hnorm_a_2, w_out_a_2, norm_kv_2,
        w_kv_2, knorm_2, norm_b_2, w_in_b_2, qnorm_b_2, w_out_b_2, ple_norm_2, w_ple_gate_2,
        w_ple_2,
    )


_drawn_inputs = setup_inputs


def setup_inputs(seed=0):
    import zlib

    import numpy as np

    out = dict(_drawn_inputs(seed))
    spreads = {}
    factors = {'attn_norm': 5.327,
     'mlp_norm': 2.79,
     'a_subln': 6.844,
     'kv_ada_b': 6.995,
     'kv_norm': 8.0,
     'cmp_pos': 4.37,
     'final_norm': 2.691,
     'norm_kv_2': 4.522,
     'knorm_2': 8.0,
     'norm_b_2': 4.578,
     'qnorm_b_2': 8.0,
     'ple_norm_2': 5.075}
    for name, (base, spread) in spreads.items():
        noise = np.random.default_rng([zlib.crc32(name.encode()), seed]).standard_normal(out[name].shape)
        drawn = base * np.exp(spread * noise) if base else spread * noise
        out[name] = __import__('jax').numpy.asarray(drawn.astype(out[name].dtype))
    for name, factor in factors.items():
        out[name] = (out[name] * factor).astype(out[name].dtype)
    return out
```

```python
import math
from contextlib import ExitStack

import numpy as np

import concourse.bass as bass
from concourse import mybir

F32 = mybir.dt.float32
F32R = mybir.dt.float32r
ALU = mybir.AluOpType
ACT = mybir.ActivationFunctionType
AX = mybir.AxisListType

P = 128
T = 512
D = 1024
KC = D // P
NT = T // P
HALF = 2048
EPS = 1e-6
NEG = -1e30
BIG = 3.0e38
BUCKETS, MAX_DIST = 32, 128
HEADS = 16
A_H = 8
HD = 64
SCALE = HD ** -0.5
LAM_INIT = 0.8 - 0.6 * math.exp(-0.3 * 0)
GRP = 4
NCMP = (T - 32) // 16 + 1
FF = 4 * D

STREAM = [("a_in", 12), ("a_out", 4), ("mlp0", 32), ("kv", 6), ("cmp0", 2), ("b_in0", 2), ("cmp1", 2), ("b_in1", 2), ("b_out", 4), ("mlp1", 32),
          ("m_in", 16), ("m_out", 4), ("ple0g", 4), ("ple0p", 1), ("kv2", 4), ("d_in", 8), ("d_out", 2),
          ("ple1g", 4), ("ple1p", 1)]
HALF0 = {}
_n = 0
for _name, _c in STREAM:
    HALF0[_name] = _n
    _n += _c
N_HALF = _n
ADA_ALL = 112
ADA_FIRST = 16

COLS = [("attn_norm", 16), ("mlp_norm", 16), ("kv_norm", 8), ("final_norm", 8), ("ada_b", 112), ("norm_a", 8),
        ("norm_kv", 8), ("norm_b", 8), ("ple_norm", 16), ("hnorm", 8), ("conv", 32), ("subln", 1),
        ("knorm", 1), ("knorm_s", 1), ("qnorm", 1), ("qnorm_s", 1), ("b_gate", 2)]
COL0 = {}
_n = 0
for _name, _c in COLS:
    COL0[_name] = _n
    _n += _c
N_COLS = _n


def bucket_of(dist):
    n = np.maximum(dist, 0)
    half = BUCKETS // 2
    nf = np.maximum(n, 1).astype(np.float32)
    large = half + (np.log(nf / np.float32(half)) / np.float32(math.log(MAX_DIST / half))
                    * np.float32(BUCKETS - half)).astype(np.int32)
    return np.where(n < half, n, np.minimum(large, BUCKETS - 1))


def constants():
    idx = np.arange(640)
    dist = (T - 1) - idx
    row = np.where(dist < 0, BUCKETS, bucket_of(dist))
    oh = (np.arange(BUCKETS + 1)[:, None] == row[None, :]).astype(np.float32)
    out = {"oh": oh, "ident": np.eye(P, dtype=np.float32),
           "flip": np.ascontiguousarray(np.eye(P, dtype=np.float32)[::-1])}
    q = np.arange(T).reshape(NT, P).T
    n = np.arange(32)
    ok = (n[None, None, :] * 16 + 31 <= q[:, :, None]) & (n[None, None, :] < NCMP)
    out["cmask"] = np.concatenate([np.where(ok, 0.0, NEG), ok.astype(np.float32)], axis=2).astype(np.float32)
    out["mmask"] = np.where(np.arange(P)[:, None] <= np.arange(P)[None, :], 0.0, NEG).astype(np.float32)
    a, b = np.arange(P)[:, None], np.arange(P)[None, :]
    near = np.where(a >= b, 0.0, NEG)
    back = np.where(P + a - b <= P, 0.0, NEG)
    far = np.where((a >= b) & ((a - b) % 4 == 0), 0.0, NEG)
    out["dmask"] = np.concatenate([back, near, near, far], axis=1).astype(np.float32)
    inv = np.float32(10000.0) ** (-np.arange(0, P, 2, dtype=np.float32) / np.float32(P))
    ang = np.arange(T, dtype=np.float32)[None, :] * inv[:, None]
    cos, sin = np.cos(ang), np.sin(ang)
    out["rope"] = np.ascontiguousarray(np.stack([np.concatenate([cos, cos]), np.concatenate([-sin, sin])], axis=1).astype(np.float32))
    return out


def tiles(w):
    k, n = w.shape
    return w.reshape(k // 512, 4, P, n // 512, 512).transpose(3, 0, 2, 1, 4).reshape(-1, P, HALF)


def mlp_tiles(w1, w2):
    out = []
    for g in range(4):
        out += [tiles(w1[:, g * D:(g + 1) * D]), tiles(w2[g * D:(g + 1) * D, :])]
    return np.concatenate(out)


def lay_out(i):
    i = {k: np.asarray(v, dtype=None) for k, v in i.items()}
    c = constants()

    def columns(v):
        return v.reshape(-1, P).T

    kv = i["w_kv"].reshape(D, 6, GRP * HD)
    cmp1 = i["cmp_w1"].reshape(2, 2, 8, P, 256).transpose(0, 1, 3, 2, 4).reshape(2, 2, P, HALF)
    b_in = tiles(i["b_w_in"][0][:, :D])
    stream = [
        tiles(i["a_w_in"][0]), tiles(i["a_w_out"][0]), mlp_tiles(i["mlp_w1"][0], i["mlp_w2"][0]),
        tiles(np.concatenate([kv[:, 0], kv[:, 1], kv[:, 2], kv[:, 4], kv[:, 3], kv[:, 5]], axis=1)),
        cmp1[0], b_in[0:2], cmp1[1], b_in[2:4], tiles(i["b_w_out"][0]), mlp_tiles(i["mlp_w1"][1], i["mlp_w2"][1]),
        tiles(i["w_in_a_2"][0][:, :4 * D]), tiles(i["w_out_a_2"][0]),
        tiles(i["w_ple_gate_2"][0]), i["w_ple_2"][0].reshape(1, 2, P, D).transpose(0, 2, 1, 3).reshape(1, P, HALF),
        tiles(i["w_kv_2"]), tiles(i["w_in_b_2"][0]), tiles(i["w_out_b_2"][0]),
        tiles(i["w_ple_gate_2"][1]), i["w_ple_2"][1].reshape(1, 2, P, D).transpose(0, 2, 1, 3).reshape(1, P, HALF),
    ]
    for (name, n), s in zip(STREAM, stream):
        assert s.shape == (n, P, HALF), (name, s.shape)
    c["wts"] = np.ascontiguousarray(np.concatenate(stream))
    ada = np.concatenate([i["ada_w"][0].T, i["ada_w"][1].T, i["kv_ada_w"].T])
    c["ada"] = np.ascontiguousarray(ada.reshape(ADA_ALL, P, D))

    def swapped(v):
        return np.concatenate([v[64:], v[:64]])

    bg = np.zeros((2, P), np.float32)
    bg[:, 0:4] = i["b_gate_a_2"][0].reshape(2, 4)
    parts = {
        "attn_norm": i["attn_norm"], "mlp_norm": i["mlp_norm"], "kv_norm": i["kv_norm"], "final_norm": i["final_norm"],
        "ada_b": np.concatenate([i["ada_b"].reshape(-1), i["kv_ada_b"]]), "norm_a": i["norm_a_2"],
        "norm_kv": i["norm_kv_2"], "norm_b": i["norm_b_2"], "ple_norm": i["ple_norm_2"], "hnorm": i["hnorm_a_2"],
        "conv": i["conv_a_2"][0], "subln": i["a_subln"], "knorm": i["knorm_2"], "knorm_s": swapped(i["knorm_2"]),
        "qnorm": i["qnorm_b_2"], "qnorm_s": swapped(i["qnorm_b_2"][0]), "b_gate": bg,
    }
    c["cols"] = np.ascontiguousarray(np.concatenate([columns(parts[n]) for n, _ in COLS], axis=1))
    assert c["cols"].shape == (P, N_COLS)
    c["x"] = np.ascontiguousarray(i["x"][0].T.reshape(KC, P, T).transpose(1, 0, 2))
    c["c"] = np.ascontiguousarray(i["c"])
    c["rel"] = np.ascontiguousarray(i["rel_bias"])
    c["lam"] = np.ascontiguousarray(i["a_lambda"])
    c["pos"] = np.ascontiguousarray(i["cmp_pos"].reshape(2, 16, P).transpose(2, 0, 1))
    w2 = i["cmp_w2"].reshape(2, 2, P, HD).transpose(2, 0, 1, 3)
    c["cw2"] = np.ascontiguousarray(np.concatenate([w2, w2], axis=3))
    c["gw"] = np.ascontiguousarray(i["b_w_in"][0][:, D:].reshape(KC, P, 48).transpose(1, 0, 2))
    gm = np.zeros((KC, P, 128), np.float32)
    gm[:, :, 0:4] = i["w_in_a_2"][0][:, 4 * D:4 * D + 4].reshape(KC, P, 4)
    gm[:, :, 32:36] = i["w_in_a_2"][0][:, 4 * D + 4:].reshape(KC, P, 4)
    c["gm"] = np.ascontiguousarray(gm.transpose(1, 0, 2))
    c["p"] = np.ascontiguousarray(i["p_2"][:, 0].transpose(0, 2, 1).reshape(2, 2, P, T).transpose(0, 2, 1, 3))
    return c


def place(nc, ctx):
    m = {}
    base = (nc.sbuf_base + 31) // 32 * 32
    size = (nc.sbuf_top - base) // 32 * 32
    ctx.enter_context(nc.sbuf_tensor("arena", [P, size // 4], F32))
    K = 1024
    reg = {}
    at = 0
    for name, kb in [("x", 16), ("h", 32), ("hid", 32), ("bias", 32), ("raw", 16), ("split", 32), ("ada", 16),
                     ("scr", 8), ("misc", 16)]:
        reg[name] = at
        at += kb * K
    reg["small"] = at

    class Small:
        top = at

    def t(name, shape, region, off=0, dt=F32):
        o = reg[region] + off
        m[name] = nc.alloc_sbuf_tensor_at(name, shape, dt, offset=base + o)
        return m[name]

    def s(name, shape, dt=F32):
        n = 4 * int(np.prod(shape[1:]))
        n = (n + 31) // 32 * 32
        assert Small.top + n <= size, ("small region is full", name, Small.top + n - size)
        m[name] = nc.alloc_sbuf_tensor_at(name, shape, dt, offset=base + Small.top)
        m[name + "_at"] = base + Small.top
        Small.top += n
        return m[name]

    t("x", [P, KC, T], "x")
    t("hH", [P, KC, T], "h", 0, F32R)
    t("hL", [P, KC, T], "h", 16 * K, F32R)
    t("raw", [P, 2, HALF], "raw")
    t("wH", [P, 2, HALF], "split", 0, F32R)
    t("wL", [P, 2, HALF], "split", 16 * K, F32R)
    t("tmp", [P, 3, T], "scr")
    t("rstd", [P, T], "scr", 6 * K)
    s("cols", [P, N_COLS])
    s("mods", [P, ADA_ALL])
    s("ident", [P, P])
    s("mean", [P, P])
    s("one", [P, 4])
    t("ada0", [P, 8, D], "h")
    t("ada1", [P, 8, D], "hid")
    t("adab", [P, 2, D], "ada")
    t("cb", [P, D], "ada", 8 * K)
    t("ce", [P, D], "misc")
    s("mstage", [P, 16])
    t("oh", [33, 640], "misc", 4 * K)
    t("rb", [33, HEADS], "misc", 7 * K)
    t("frow", [HEADS, 640], "misc", 8 * K)
    t("bt", [P, HEADS, T], "bias")
    t("qT", [P, A_H, T], "hid")
    t("kT", [P, A_H, T], "hid", 16 * K)
    t("vA", [P, NT, D], "misc")
    t("sA", [P, 2, T], "scr")
    t("pA0", [P, 2, T], "scr", 4 * K)
    t("pA1", [P, 2, T], "ada")
    t("ptA", [P, 2, T], "ada", 4 * K)
    t("oA", [P, 2, A_H, P], "ada", 8 * K)
    s("nm", [P, 64])
    s("rs", [P, 64])
    s("cc", [P, 4, 4])
    s("ssq", [P, 32])
    t("lamb", [P, 4, HD], "misc", 11 * K)
    t("aH", [P, KC, T], "hid", 0, F32R)
    t("aL", [P, KC, T], "hid", 16 * K, F32R)
    t("relu", [P, 4, T], "scr")
    t("kv2", [P, 2, GRP, T], "hid")
    t("kd", [P, 2, GRP, T], "hid", 16 * K)
    t("vB", [P, NT, 512], "misc")
    t("fH", [P, 16, GRP * NCMP], "ada", 0, F32R)
    t("fL", [P, 16, GRP * NCMP], "ada", 8 * K, F32R)
    t("fF", [P, 16, GRP * NCMP], "ada", 8 * K)
    t("gx", [P, 2, 2, P], "misc", 8 * K)
    t("gt", [P, 2, P], "misc", 10 * K)
    t("vblk", [P, GRP, 4 * HD], "misc", 8 * K)
    t("kcd", [P, P], "misc", 12 * K)
    t("gate", [P, NT, HEADS, 3], "misc", 12 * K + 512)
    t("cmask", [P, NT, 64], "misc", 13 * K + 256)
    t("gw", [P, KC, 48], "misc", 14 * K + 256)
    t("gwH", [P, KC, 48], "ada", 0, F32R)
    t("gwL", [P, KC, 48], "ada", 2 * K, F32R)
    t("yr", [P, 2, GRP, P], "ada", 4 * K)
    s("cw2", [P, 2, 2, P])
    s("pos", [P, 2, 16])
    t("oB", [P, 2, GRP, 4 * HD], "ada")
    t("ptB", [P, 2, T], "ada", 8 * K)
    t("sc", [P, HEADS, 32], "ada", 12 * K)
    t("ptc", [P, GRP * P], "ada", 14 * K)
    t("sB", [P, 2, T], "scr")
    t("pB", [P, 2, T], "scr", 4 * K)
    s("cx", [P, 4, 16])
    s("wr", [P, 4, 4])
    t("ot", [P, 4 * HD], "misc", 14 * K + 256)
    m["flip"] = nc.alloc_sbuf_tensor_at("flip", [P, P], F32, offset=m["cw2_at"])
    s("ones", [P, 1])
    t("gm", [P, KC, P], "misc")
    t("gmH", [P, KC, P], "misc", 4 * K, F32R)
    t("gmL", [P, KC, P], "misc", 8 * K, F32R)
    t("qkM", [P, KC, T], "hid")
    t("xc", [P, 2, T + 4], "hid", 16 * K)
    t("rows", [4, 4, T], "hid", 24 * K)
    t("wt", [P, 2, NT, T], "hid", 16 * K)
    t("vM", [P, NT, D], "ada")
    t("oM", [P, NT, D], "bias")
    t("zM", [P, NT, D], "bias", 16 * K)
    t("negM", [P, 4, T], "misc")
    t("negD", [P, 4, NT, P], "misc", 8 * K)
    t("yM", [P, 2, NT, 256], "scr")
    m["mmask"] = nc.alloc_sbuf_tensor_at("mmask", [P, P], F32, offset=m["cw2_at"])
    t("sg", [P, KC, T], "hid")
    t("pF", [P, 2, T], "misc")
    t("pH", [P, 2, T], "misc", 4 * K, F32R)
    t("pL", [P, 2, T], "misc", 8 * K, F32R)
    m["dmask"] = nc.alloc_sbuf_tensor_at("dmask", [P, T], F32, offset=m["cw2_at"])
    t("rope", [P, 2, T], "misc", 12 * K)
    t("qD", [P, 12, T], "hid")
    t("kD", [P, 4, T], "hid", 24 * K)
    t("vD", [P, NT, T], "bias")
    t("vC", [P, 4, T], "bias", 8 * K)
    t("zD", [P, 4, T], "bias", 16 * K)
    t("rpK", [P, 2, T], "bias", 24 * K)
    t("rpQ", [P, 2, T], "bias", 28 * K)
    t("rw", [P, 4, T], "ada")
    t("sw", [P, 4, T], "ada", 8 * K)
    t("hq", [P, 2, T], "misc", 4 * K)
    t("hr", [P, 2, T], "misc", 8 * K)
    t("sD", [P, 2, 256], "misc")
    t("pD", [P, 2, 256], "misc", 2 * K)
    t("ptD", [P, 2, 256], "misc", 4 * K)
    t("nmR", [4, 3, T], "scr")
    t("nmS", [4, T], "scr", 6 * K)
    t("rsR", [4, 3, T], "misc", 8 * K)
    t("zR", [4, T], "misc", 14 * K)
    t("hz", [P, 2, T], "misc", 12 * K)
    return m


def program(nc, d, out):
    ctx = ExitStack()
    with ctx:
        sb = place(nc, ctx)
        x, hH, hL, raw, wH, wL, tmp, rstd = (sb[n] for n in ("x", "hH", "hL", "raw", "wH", "wL", "tmp", "rstd"))
        cols, mods, ident, one = sb["cols"], sb["mods"], sb["ident"], sb["one"]
        bank = ctx.enter_context(nc.psum_tensor("bank", [P, 8, T], F32))
        fscr = nc.dram_tensor("bias_rows", (HEADS, 640), F32, kind="Internal").ap()
        sems = {}

        def sem(name):
            if name not in sems:
                sems[name] = ctx.enter_context(nc.semaphore(name))
            return sems[name]

        raw_in = [sem(f"raw_in{i}") for i in range(2)]
        w_hi, w_lo = sem("w_hi"), sem("w_lo")
        half_used = sem("half_used")
        acc_free = [sem(f"acc_free{i}") for i in range(2)]
        ada_in = [sem(f"ada_in{i}") for i in range(2)]
        ada_used = sem("ada_used")
        par_in, x_in = sem("par_in"), sem("x_in")
        sq_done, stat_mm, ln_done, rstd_done = sem("sq_done"), sem("stat_mm"), sem("ln_done"), sem("rstd_done")
        tmp_done, hf_done, h_hi, h_lo = sem("tmp_done"), sem("hf_done"), sem("h_hi"), sem("h_lo")
        ready = sem("ready")
        silu_e, cb_ready = sem("silu_e"), sem("cb_ready")
        mod_ready = sem("mod_ready")
        f_mm, f_row, f_out, bt_in, bt_mm, bt_out = (
            sem("f_mm"), sem("f_row"), sem("f_out"), sem("bt_in"), sem("bt_mm"), sem("bt_out"))
        lam_s, lam_e, lam_ready = sem("lam_s"), sem("lam_e"), sem("lam_ready")
        out_done = sem("out_done")

        def col(name, c=0):
            return cols[:, COL0[name] + c:COL0[name] + c + 1]

        def mod(c):
            return mods[:, c:c + 1]

        def hi(act, n):
            act.wait_ge(raw_in[n % 2], 16 * (n // 2 + 1))
            if n >= 2:
                act.wait_ge(half_used, n - 1)
            act.activation(wH[:, n % 2, :], raw[:, n % 2, :], ACT.Copy).then_inc(w_hi, 1)

        def lo(dve, n):
            dve.wait_ge(w_hi, n + 1)
            dve.tensor_tensor(wL[:, n % 2, :], raw[:, n % 2, :], wH[:, n % 2, :].bitcast(F32),
                              ALU.subtract).then_inc(w_lo, 1)

        def acc_wait(pe, a):
            if a >= 2:
                pe.wait_ge(acc_free[a % 2], 4 * (a // 2))

        def evac(eng, a, m):
            return bank[:, 4 * (a % 2) + m, :], acc_free[a % 2]

        def three(pe, o, l, r, start, stop):
            pe.matmul(o, l[0], r[0], start=start, stop=False)
            pe.matmul(o, l[0], r[1], start=False, stop=False)
            return pe.matmul(o, l[1], r[0], start=False, stop=stop)

        def wpart(s, k, c0, n, width=512):
            a = k * width + c0
            return wH[:, s, a:a + n], wL[:, s, a:a + n]

        def tile_mm(pe, a, n0, xs=None, tok=False, hbase=None):
            xh, xl = xs or (hH, hL)
            acc_wait(pe, a)
            for j in range(2):
                pe.wait_ge(w_lo, n0 + j + 1)
                s = (n0 + j) % 2
                for kk in range(4):
                    k = 4 * j + kk
                    if hbase is not None:
                        pe.wait_ge(h_lo, hbase + k + 1)
                    for m in range(4):
                        o = bank[:, 4 * (a % 2) + m, :]
                        if tok:
                            l = (xh[:, k, m * P:(m + 1) * P], xl[:, k, m * P:(m + 1) * P])
                            r = wpart(s, kk, 0, 512)
                        else:
                            l, r = wpart(s, kk, m * P, P), (xh[:, k, :], xl[:, k, :])
                        last = three(pe, o, l, r, k == 0, k == KC - 1)
                last.then_inc(half_used, 1)

        def stats_act(act, s, xwait, next_a):
            for c in range(KC):
                q = KC * s + c
                xwait(act, c)
                if c >= 3:
                    act.wait_ge(stat_mm, q - 2)
                act.activation(tmp[:, c % 3, :], x[:, c, :], ACT.Square).then_inc(sq_done, 1)
            act.wait_ge(stat_mm, KC * s + KC)
            act.activation(rstd[:, :], bank[:, 4 * (next_a % 2), :], ACT.Ln, bias=one[:, 1:2]).then_inc(ln_done, 1)
            act.wait_ge(ln_done, s + 1)
            act.activation(rstd[:, :], rstd[:, :], ACT.Exp, scale=-0.5).then_inc(rstd_done, 1)

        def stats_pe(pe, s, next_a):
            acc_wait(pe, next_a)
            if s == 0:
                pe.wait_ge(ready, 1)
            for c in range(KC):
                pe.wait_ge(sq_done, KC * s + c + 1)
                pe.matmul(bank[:, 4 * (next_a % 2), :], sb["mean"][:, :], tmp[:, c % 3, :],
                          start=(c == 0), stop=(c == KC - 1)).then_inc(stat_mm, 1)

        def apply_dve(dve, p, s):
            def product(c):
                dve.tensor_tensor(tmp[:, c % 3, :], x[:, c, :], rstd[:, :], ALU.mult).then_inc(tmp_done, 1)

            def rest(c):
                dve.wait_ge(h_hi, KC * p + c + 1)
                dve.tensor_tensor(hL[:, c, :], tmp[:, c % 3, :], hH[:, c, :].bitcast(F32),
                                  ALU.subtract).then_inc(h_lo, 1)

            dve.wait_ge(rstd_done, s + 1)
            product(0)
            product(1)
            for c in range(KC):
                if c + 2 < KC:
                    if c >= 1:
                        dve.wait_ge(h_lo, KC * p + c)
                    product(c + 2)
                rest(c)

        def apply_act(act, p, scale, shift, free=None):
            for c in range(KC):
                q = KC * p + c
                act.wait_ge(tmp_done, q + 1)
                b = shift(c) if shift else 0.0
                act.activation(tmp[:, c % 3, :], tmp[:, c % 3, :], ACT.Identity, bias=b,
                               scale=scale(c)).then_inc(hf_done, 1)
                act.wait_ge(hf_done, q + 1)
                if c == 0 and free:
                    free(act)
                act.activation(hH[:, c, :], tmp[:, c % 3, :], ACT.Copy).then_inc(h_hi, 1)

        def xw_loaded(eng, c):
            eng.wait_ge(x_in, 16)

        def xw_evac(a0):
            def w(eng, c):
                a = a0 + c // 4
                eng.wait_ge(acc_free[a % 2], 4 * (a // 2) + c % 4 + 1)
            return w

        def residual_dve(dve, a, c0, gate):
            for m in range(4):
                o, freed = evac(dve, a, m)
                if gate is None:
                    dve.tensor_tensor(x[:, c0 + m, :], o, x[:, c0 + m, :], ALU.add).then_inc(freed, 1)
                    continue
                dve.scalar_tensor_tensor(out=x[:, c0 + m, :], in0=o, scalar=gate(c0 + m), in1=x[:, c0 + m, :],
                                         op0=ALU.mult, op1=ALU.add).then_inc(freed, 1)

        def ada_sum(dve, slot, dst):
            return dve.tensor_tensor_reduce(slot, slot, sb["cb"][:, :], 1.0, 0.0, ALU.mult, ALU.add, dst)

        def ada_dve(dve, k, dst=None):
            j = k - ADA_FIRST
            dve.wait_ge(ada_in[j % 2], 16 * (j // 2 + 1))
            ada_sum(dve, sb["adab"][:, j % 2, :], mod(k) if dst is None else dst).then_inc(ada_used, 1)

        def ada_load(sp, k):
            j = k - ADA_FIRST
            if j >= 2:
                sp.wait_ge(ada_used, j - 1)
            sp.dma_start(sb["adab"][:, j % 2, :], d["ada"][k]).then_inc(ada_in[j % 2], 16)

        def load_half(sp, n):
            if n >= N_HALF:
                return
            if n >= 2:
                sp.wait_ge(w_lo, n - 1)
            sp.dma_start(raw[:, n % 2, :], d["wts"][n]).then_inc(raw_in[n % 2], 16)

        block = ctx.enter_context(nc.Block())

        A_TILE = {"a_in": 0, "a_out": 6, "mlp0": 8, "kv": 24, "b_in": 27, "b_out": 29, "mlp1": 31, "m_in": 47,
                  "m_out": 55, "ple0g": 57, "ple0p": 59, "kv2": 61, "d_in": 63, "d_out": 67, "ple1g": 69, "ple1p": 71}

        s_mm, s_max, p_exp, p_ratio, p_mix, t_mm, t_out, o_mm, o_out, o_sq = (sem(n) for n in (
            "s_mm", "s_max", "p_exp", "p_ratio", "p_mix", "t_mm", "t_out", "o_mm", "o_out", "o_sq"))
        r_ln, r_exp, o_norm, p_inv = (sem(n) for n in ("r_ln", "r_exp", "o_norm", "p_inv"))
        y_t, y_hi, y_lo = (sem(n) for n in ("y_t", "y_hi", "y_lo"))
        qT, kT, vA, sA, ptA, oA = (sb[n] for n in ("qT", "kT", "vA", "sA", "ptA", "oA"))
        pA = [sb["pA0"], sb["pA1"]]
        nm, rs, cc, ssq = sb["nm"], sb["rs"], sb["cc"], sb["ssq"]
        PAIRS = NT * A_H

        def pslot(u, w):
            return pA[(u // 2) % 2][:, u % 2, 0:w]

        def diff_pe(pe):
            pe.wait_ge(acc_free[1], 4 * 3)
            pe.wait_ge(acc_free[0], 4 * 3)

            def scores(v):
                i, h = divmod(v, A_H)
                w = (i + 1) * P
                for m in range(2):
                    u = 2 * v + m
                    if u >= 3:
                        pe.wait_ge(s_max, u - 2)
                    pe.matmul(bank[:, u % 3, 0:w], qT[m * HD:(m + 1) * HD, h, i * P:(i + 1) * P],
                              kT[m * HD:(m + 1) * HD, h, 0:w], start=True, stop=True).then_inc(s_mm, 1)

            def turn(v):
                i = v // A_H
                pe.wait_ge(p_mix, v + 1)
                if v >= 2:
                    pe.wait_ge(t_out, v - 1)
                for j in range(i + 1):
                    last = pe.transpose(bank[:, 3 + v % 2, j * P:(j + 1) * P],
                                        pslot(2 * v, T)[:, j * P:(j + 1) * P], ident[:, :])
                last.then_inc(t_mm, 1)

            def values(v):
                i, h = divmod(v, A_H)
                pe.wait_ge(t_out, v + 1)
                if v >= 2:
                    pe.wait_ge(o_sq, v - 1)
                for j in range(i + 1):
                    last = pe.matmul(bank[:, 5 + v % 2, 0:P], ptA[:, v % 2, j * P:(j + 1) * P],
                                     vA[:, j, h * P:(h + 1) * P], start=(j == 0), stop=(j == i))
                last.then_inc(o_mm, 1)

            def tail(i, r):
                e = 2 * i + r
                pe.wait_ge(o_norm, i + 1)
                if e >= 1:
                    pe.wait_ge(y_lo, e)
                for h in range(4):
                    last = pe.transpose(bank[:, 7, h * P:(h + 1) * P], oA[:, i % 2, 4 * r + h, :], ident[:, :])
                last.then_inc(y_t, 1)

            scores(0)
            for v in range(PAIRS + 6):
                if v + 1 < PAIRS:
                    scores(v + 1)
                if 2 <= v < PAIRS + 2:
                    values(v - 2)
                if v < PAIRS:
                    turn(v)
                for i in range(NT):
                    for r in range(2):
                        if v == A_H * i + 11 + 2 * r:
                            tail(i, r)

        def diff_dve(dve):
            dve.wait_ge(bt_out, HEADS)
            dve.wait_ge(lam_ready, 2)

            def bias_max(v):
                i, h = divmod(v, A_H)
                w = (i + 1) * P
                for m in range(2):
                    u = 2 * v + m
                    dve.wait_ge(s_mm, u + 1)
                    if u >= 2:
                        dve.wait_ge(p_exp, u - 1)
                    dve.tensor_tensor_reduce(sA[:, m, 0:w], bank[:, u % 3, 0:w],
                                             sb['bt'][:, 2 * h + m, T - w:T], -SCALE, BIG, ALU.add, ALU.min,
                                             nm[:, u:u + 1]).then_inc(s_max, 1)

            def mix(v):
                i = v // A_H
                w = (i + 1) * P
                dve.wait_ge(p_exp, 2 * v + 2)
                c = cc[:, v % 4, :]
                if v >= 4:
                    dve.wait_ge(o_sq, v - 3)
                dve.reciprocal(c[:, 0:2], rs[:, 2 * v:2 * v + 2]).then_inc(p_inv, 1)
                dve.wait_ge(p_inv, v + 1)
                dve.scalar_tensor_tensor(out=c[:, 3:4], in0=rs[:, 2 * v:2 * v + 1], scalar=one[:, 2:3],
                                         in1=c[:, 1:2], op0=ALU.mult, op1=ALU.mult).then_inc(p_ratio, 1)
                dve.wait_ge(p_ratio, v + 1)
                dve.scalar_tensor_tensor(out=pslot(2 * v, w), in0=pslot(2 * v + 1, w), scalar=c[:, 3:4],
                                         in1=pslot(2 * v, w), op0=ALU.mult, op1=ALU.add).then_inc(p_mix, 1)

            def norm(i):
                dve.wait_ge(r_exp, i + 1)
                dve.wait_ge(o_out, A_H * (i + 1))
                o = oA[:, i % 2, :, :]
                dve.tensor_tensor(o, o, ssq[:, i * A_H:(i + 1) * A_H].rearrange("p (h o) -> p h o", o=1)
                                  .to_broadcast([P, A_H, P]), ALU.mult).then_inc(o_norm, 1)

            def tail(i, r):
                dve.wait_ge(y_hi, 2 * i + r + 1)
                dve.scalar_tensor_tensor(
                    out=hL[:, 4 * r:4 * r + 4, i * P:(i + 1) * P],
                    in0=bank[:, 7, :].rearrange("p (h q) -> p h q", h=4), scalar=one[:, 3:4],
                    in1=hH[:, 4 * r:4 * r + 4, i * P:(i + 1) * P].bitcast(F32),
                    op0=ALU.mult, op1=ALU.subtract).then_inc(y_lo, 1)

            bias_max(0)
            for v in range(PAIRS + 7):
                if v + 1 < PAIRS:
                    bias_max(v + 1)
                if v < PAIRS:
                    mix(v)
                for i in range(NT):
                    if v == A_H * i + 10:
                        norm(i)
                    for r in range(2):
                        if v == A_H * i + 12 + 2 * r:
                            tail(i, r)

        def diff_act(act):
            def exps(v):
                w = (v // A_H + 1) * P
                for m in range(2):
                    u = 2 * v + m
                    act.wait_ge(s_max, u + 1)
                    if u >= 4:
                        act.wait_ge(t_mm, u // 2 - 1)
                    act.activation(pslot(u, w), sA[:, m, 0:w], ACT.Exp, bias=nm[:, u:u + 1], scale=-1.0,
                                   accum_out=rs[:, u:u + 1]).then_inc(p_exp, 1)

            def copy_out(v):
                w = (v // A_H + 1) * P
                act.wait_ge(t_mm, v + 1)
                act.activation(ptA[:, v % 2, 0:w], bank[:, 3 + v % 2, 0:w], ACT.Copy).then_inc(t_out, 1)

            def copy_o(v):
                i, h = divmod(v, A_H)
                act.wait_ge(p_inv, v + 1)
                act.wait_ge(o_mm, v + 1)
                if i >= 2 and h == 0:
                    act.wait_ge(y_t, 2 * (i - 1))
                o = bank[:, 5 + v % 2, 0:P]
                act.activation(oA[:, i % 2, h, :], o, ACT.Copy, scale=cc[:, v % 4, 0:1]).then_inc(o_out, 1)
                act.wait_ge(o_out, v + 1)
                act.activation(o, o, ACT.Square, scale=cc[:, v % 4, 0:1],
                               accum_out=ssq[:, v:v + 1]).then_inc(o_sq, 1)

            def rstds(i):
                r = ssq[:, i * A_H:(i + 1) * A_H]
                act.wait_ge(o_sq, A_H * (i + 1))
                act.activation(r, r, ACT.Ln, bias=one[:, 1:2], scale=1.0 / P).then_inc(r_ln, 1)
                act.wait_ge(r_ln, i + 1)
                act.activation(r, r, ACT.Exp, scale=-0.5).then_inc(r_exp, 1)

            def tail(i, r):
                act.wait_ge(y_t, 2 * i + r + 1)
                act.activation(hH[:, 4 * r:4 * r + 4, i * P:(i + 1) * P],
                               bank[:, 7, :].rearrange("p (h q) -> p h q", h=4), ACT.Copy,
                               scale=one[:, 3:4]).then_inc(y_hi, 1)

            exps(0)
            for v in range(PAIRS + 6):
                if v + 1 < PAIRS:
                    exps(v + 1)
                if 2 <= v < PAIRS + 2:
                    copy_o(v - 2)
                if v < PAIRS:
                    copy_out(v)
                for i in range(NT):
                    if v == A_H * i + 9:
                        rstds(i)
                    for r in range(2):
                        if v == A_H * i + 11 + 2 * r:
                            tail(i, r)

        hid_hi, hid_sq, hid_lo = sem("hid_hi"), sem("hid_sq"), sem("hid_lo")
        aH, aL, relu = sb["aH"], sb["aL"], sb["relu"]
        mst = sem("mst")

        def mlp_pe(pe, layer, hbase):
            n0, a0, b0 = HALF0[f"mlp{layer}"], A_TILE[f"mlp{layer}"], 4 * KC * layer
            pe.wait_ge(h_lo, hbase)
            with pe.Fori(0, 4) as g:
                for q in range(4):
                    st = (a0 + q) % 2
                    pe.wait_ge(acc_free[st], g * 8 + 4 * ((a0 + q) // 2))
                    for j in range(2):
                        nn = 2 * q + j
                        pe.wait_ge(w_lo, g * 8 + (n0 + nn + 1))
                        for kk in range(4):
                            k = 4 * j + kk
                            if q == 2:
                                pe.wait_ge(hid_lo, g * 8 + (b0 + k + 1))
                            for m in range(4):
                                xs = (hH, hL) if q < 2 else (aH, aL)
                                last = three(pe, bank[:, 4 * st + m, :], wpart((n0 + nn) % 2, kk, m * P, P),
                                             (xs[0][:, k, :], xs[1][:, k, :]), k == 0, k == KC - 1)
                        last.then_inc(half_used, 1)

        def mlp_act(act, layer):
            n0, a0, b0 = HALF0[f"mlp{layer}"], A_TILE[f"mlp{layer}"], 4 * KC * layer
            with act.Fori(0, 4) as g:
                for q in range(4):
                    for j in range(2):
                        n = n0 + 2 * q + j + 2
                        act.wait_ge(raw_in[n % 2], g * 64 + 16 * (n // 2 + 1))
                        act.wait_ge(half_used, g * 8 + (n - 1))
                        act.activation(wH[:, n % 2, :], raw[:, n % 2, :], ACT.Copy).then_inc(w_hi, 1)
                    if q >= 2:
                        continue
                    st = (a0 + q) % 2
                    act.wait_ge(half_used, g * 8 + (n0 + 2 * q + 2))
                    if q == 1:
                        act.wait_ge(hid_lo, g * 8 + (b0 + 4))
                    for m in range(4):
                        act.activation(relu[:, m, :], bank[:, 4 * st + m, :], ACT.Relu).then_inc(acc_free[st], 1)
                    for m in range(4):
                        act.wait_ge(acc_free[st], g * 8 + (4 * ((a0 + q) // 2) + m + 1))
                        act.activation(aH[:, 4 * q + m, :], relu[:, m, :], ACT.Square).then_inc(hid_hi, 1)

        def mlp_dve(dve, layer):
            n0, a0, b0 = HALF0[f"mlp{layer}"], A_TILE[f"mlp{layer}"], 4 * KC * layer
            with dve.Fori(0, 4) as g:
                for q in range(4):
                    for j in range(2):
                        n = n0 + 2 * q + j + 2
                        dve.wait_ge(w_hi, g * 8 + (n + 1))
                        dve.tensor_tensor(wL[:, n % 2, :], raw[:, n % 2, :], wH[:, n % 2, :].bitcast(F32),
                                          ALU.subtract).then_inc(w_lo, 1)
                        if layer == 0 and j == 0:
                            for r in range(4):
                                c = 4 * q + r
                                dve.wait_ge(ada_in[c % 2], g * 128 + 16 * ((32 + c) // 2 + 1))
                                if c == 0:
                                    dve.wait_ge(mst, g + 1)
                                ada_sum(dve, sb["adab"][:, c % 2, :], sb["mstage"][:, c:c + 1]).then_inc(ada_used, 1)
                    st = (a0 + q) % 2
                    if q < 2:
                        for m in range(4):
                            dve.wait_ge(hid_hi, g * 8 + (b0 + 4 * q + m + 1))
                            dve.tensor_tensor(relu[:, m, :], relu[:, m, :], relu[:, m, :], ALU.mult).then_inc(hid_sq, 1)
                        for m in range(4):
                            dve.wait_ge(hid_sq, g * 8 + (b0 + 4 * q + m + 1))
                            dve.tensor_tensor(aL[:, 4 * q + m, :], relu[:, m, :], aH[:, 4 * q + m, :].bitcast(F32),
                                              ALU.subtract).then_inc(hid_lo, 1)
                    else:
                        dve.wait_ge(half_used, g * 8 + (n0 + 2 * q + 2))
                        residual_dve(dve, a0 + q, 4 * (q - 2), lambda c: mod(48 * layer + 40 + c))
                if layer == 0:
                    dve.wait_ge(ada_used, g * 16 + 48)
                    dve.tensor_tensor(mods[:, bass.ds(g * 16 + 48, 16)], sb["mstage"][:, :],
                                      cols[:, bass.ds(g * 16 + (COL0["ada_b"] + 48), 16)], ALU.add).then_inc(mst, 1)

        def mlp_sp(sp, layer):
            n0 = HALF0[f"mlp{layer}"]
            with sp.Fori(0, 4) as g:
                for nn in range(8):
                    n = n0 + nn + 2
                    sp.wait_ge(w_lo, g * 8 + (n - 1))
                    sp.dma_start(raw[:, n % 2, :], d["wts"][bass.ds(g * 8 + n, 1)].rearrange("o p n -> (o p) n"))\
                        .then_inc(raw_in[n % 2], 16)
                    if layer == 0:
                        for r in range(2):
                            c = 2 * nn + r
                            sp.wait_ge(ada_used, g * 16 + (32 + c - 1))
                            sp.dma_start(sb["adab"][:, c % 2, :],
                                         d["ada"][bass.ds(g * 16 + (48 + c), 1)].rearrange("o p n -> (o p) n"))\
                                .then_inc(ada_in[c % 2], 16)

        def mod_cols(dve, c0, n, step):
            dve.tensor_tensor(mods[:, c0:c0 + n], mods[:, c0:c0 + n], cols[:, COL0["ada_b"] + c0:COL0["ada_b"] + c0 + n],
                              ALU.add).then_inc(mod_ready, 1)
            dve.wait_ge(mod_ready, step + 1)

        def mod_scale(dve, c0, gain):
            g = COL0[gain[0]] + gain[1]
            dve.scalar_tensor_tensor(out=mods[:, c0:c0 + KC], in0=mods[:, c0:c0 + KC], scalar=1.0,
                                     in1=cols[:, g:g + KC], op0=ALU.add, op1=ALU.mult).then_inc(mod_ready, 1)

        csave = nc.dram_tensor("silu_row", (1, D), F32, kind="Internal").ap()
        par2_in = sem("par2_in")
        c_saved, cb_back = sem("c_saved"), sem("cb_back")
        ada_h = [sem("ada_h0"), sem("ada_h1")]
        ada_pre = sem("ada_pre")

        def sp_first(sp):
            sp.dma_start(sb["cb"][:, :], d["c"].to_broadcast([P, D])).then_inc(cb_back, 16)
            sp.dma_start(x[:, :, :], d["x"]).then_inc(x_in, 16)
            for g in range(2):
                sp.dma_start(sb[f"ada{g}"][:, :, :], d["ada"][8 * g:8 * g + 8].rearrange("k p n -> p k n"))\
                    .then_inc(ada_h[g], 16)
            load_half(sp, 0)
            load_half(sp, 1)
            sp.wait_ge(f_row, 2)
            sp.dma_start(fscr, sb["frow"][:, :]).then_inc(f_out, 16)
            sp.wait_ge(f_out, 16)
            skewed = bass.AP(tensor=fscr.tensor, offset=0, ap=[[1, P], [640, HEADS], [1, T]])
            sp.dma_start(sb["bt"][:, :, :], skewed).then_inc(bt_in, 16)
            sp.wait_ge(cb_ready, 3)
            sp.dma_start(csave, sb["cb"][0:1, :]).then_inc(c_saved, 16)
            for n in range(12):
                load_half(sp, n + 2)
                ada_load(sp, 16 + 2 * n)
                ada_load(sp, 17 + 2 * n)
            sp.wait_ge(c_saved, 16)
            sp.wait_ge(y_lo, 8)
            sp.dma_start(sb["cb"][:, :], csave.to_broadcast([P, D])).then_inc(cb_back, 16)
            for name in ("cw2", "pos", "gw", "cmask"):
                sp.dma_start(sb[name].ap(), d[name]).then_inc(par2_in, 16)
            for n in range(12, 16):
                load_half(sp, n + 2)
                ada_load(sp, 16 + 2 * n)
                ada_load(sp, 17 + 2 * n)

        def act_first(act):
            for name, dst in (("cols", cols[:, :]), ("ident", ident[:, :]), ("oh", sb["oh"][:, :]),
                              ("rel", sb["rb"][0:BUCKETS, :]), ("flip", sb["flip"][:, :]), ("lam", None)):
                if name == "lam":
                    act.dma_start(sb["lamb"][:, :, :], d["lam"].to_broadcast([P, 4, HD])).then_inc(par_in, 16)
                else:
                    act.dma_start(dst, d[name]).then_inc(par_in, 16)
            act.wait_ge(cb_back, 16)
            act.activation(sb["ce"][:, :], sb["cb"][:, :], ACT.Exp, scale=-1.0).then_inc(silu_e, 1)
            for r in range(2):
                act.wait_ge(f_mm, r + 1)
                w = (T, P)[r]
                act.activation(sb["frow"][:, r * T:r * T + w], bank[0:HEADS, 6 + r, 0:w], ACT.Copy,
                               scale=1.0 / SCALE).then_inc(f_row, 1)
            act.wait_ge(lam_s, 2)
            act.activation(cc[:, 0, 2:4], cc[:, 0, 0:2], ACT.Exp).then_inc(lam_e, 1)
            hi(act, 0)
            hi(act, 1)
            stats_act(act, 0, xw_loaded, 0)
            act.wait_ge(mod_ready, 2)
            apply_act(act, 0, lambda c: mod(8 + c), lambda c: mod(c))
            act.wait_ge(f_out, 16)
            act.wait_ge(lam_ready, 2)
            for a in range(6):
                hi(act, 2 * a + 2)
                hi(act, 2 * a + 3)
                act.wait_ge(half_used, 2 * a + 2)
                for m in range(4):
                    o, freed = evac(act, a, m)
                    dst = (qT[:, 4 * a + m, :] if a < 2 else kT[:, 4 * (a - 2) + m, :] if a < 4
                           else vA[:, m, (a - 4) * T:(a - 3) * T])
                    act.activation(dst, o, ACT.Copy).then_inc(freed, 1)
                if a == 3:
                    for h in range(HEADS):
                        act.wait_ge(bt_mm, h + 1)
                        act.activation(sb["bt"][:, h, :], bank[:, h % 4, :], ACT.Copy).then_inc(bt_out, 1)
            diff_act(act)
            for a in (6, 7):
                hi(act, 2 * a + 2)
                hi(act, 2 * a + 3)
            stats_act(act, 1, xw_evac(6), 8)
            act.wait_ge(mod_ready, 5)
            apply_act(act, 1, lambda c: mod(32 + c), lambda c: mod(24 + c))
            mlp_act(act, 0)

        def dve_first(dve):
            for dst, value in ((sb["mean"][:, :], 1.0 / D), (one[:, 1:2], EPS), (sb["rb"][32:33, :], NEG),
                               (one[:, 0:1], 0.0)):
                dve.memset(dst, value).then_inc(ready, 1)
            dve.memset(sb["mstage"][:, :], 0.0).then_inc(mst, 1)
            dve.wait_ge(silu_e, 1)
            ce, cb = sb["ce"][:, :], sb["cb"][:, :]
            dve.tensor_scalar(ce, ce, 1.0, None, ALU.add).then_inc(cb_ready, 1)
            dve.wait_ge(cb_ready, 1)
            dve.reciprocal(ce, ce).then_inc(cb_ready, 1)
            dve.wait_ge(cb_ready, 2)
            dve.tensor_tensor(cb, cb, ce, ALU.mult).then_inc(cb_ready, 1)
            dve.wait_ge(cb_ready, 3)
            dve.wait_ge(par_in, 96)
            for r in range(2):
                l = sb["lamb"]
                dve.tensor_tensor_reduce(l[:, 2 * r, :], l[:, 2 * r, :], l[:, 2 * r + 1, :], 1.0, 0.0,
                                         ALU.mult, ALU.add, cc[:, 0, r:r + 1]).then_inc(lam_s, 1)
            dve.wait_ge(lam_e, 1)
            dve.tensor_tensor(one[:, 2:3], cc[:, 0, 3:4], cc[:, 0, 2:3], ALU.subtract).then_inc(lam_s, 1)
            dve.wait_ge(lam_s, 3)
            dve.tensor_scalar(one[:, 2:3], one[:, 2:3], -LAM_INIT, None, ALU.add).then_inc(lam_ready, 1)
            dve.tensor_scalar(one[:, 3:4], col("subln"), 1.0 - LAM_INIT, None, ALU.mult).then_inc(lam_ready, 1)
            lo(dve, 0)
            lo(dve, 1)
            for g in range(2):
                dve.wait_ge(ada_h[g], 16)
                for k in range(8):
                    ada_sum(dve, sb[f"ada{g}"][:, k, :], mod(8 * g + k)).then_inc(ada_pre, 1)
            dve.wait_ge(ada_pre, 16)
            mod_cols(dve, 0, 16, 0)
            mod_scale(dve, 8, ("attn_norm", 0))
            apply_dve(dve, 0, 0)
            for n in range(12):
                lo(dve, n + 2)
                ada_dve(dve, 16 + 2 * n)
                ada_dve(dve, 17 + 2 * n)
            diff_dve(dve)
            dve.wait_ge(ada_used, 24)
            mod_cols(dve, 16, 24, 2)
            mod_scale(dve, 32, ("mlp_norm", 0))
            dve.wait_ge(cb_back, 32)
            for a in (6, 7):
                lo(dve, 2 * a + 2)
                for k in range(4):
                    ada_dve(dve, 40 + 4 * (a - 6) + k)
                lo(dve, 2 * a + 3)
                dve.wait_ge(half_used, 2 * a + 2)
                residual_dve(dve, a, 4 * (a - 6), lambda c: mod(16 + c))
            dve.wait_ge(ada_used, 32)
            mod_cols(dve, 40, 8, 4)
            apply_dve(dve, 1, 1)
            mlp_dve(dve, 0)

        def pe_first(pe):
            pe.wait_ge(ready, 4)
            pe.wait_ge(par_in, 96)
            pe.matmul(bank[0:HEADS, 6, :], sb["rb"][:, :], sb["oh"][:, 0:T], start=True, stop=True).then_inc(f_mm, 1)
            pe.matmul(bank[0:HEADS, 7, 0:P], sb["rb"][:, :], sb["oh"][:, T:640], start=True, stop=True).then_inc(f_mm, 1)
            stats_pe(pe, 0, 0)
            for a in range(6):
                if a == 4:
                    pe.wait_ge(bt_in, 16)
                    acc_wait(pe, 4)
                    for h in range(HEADS):
                        if h >= 4:
                            pe.wait_ge(bt_out, h - 3)
                        pe.matmul(bank[:, h % 4, :], sb["flip"][:, :], sb["bt"][:, h, :], start=True, stop=True)\
                            .then_inc(bt_mm, 1)
                    pe.wait_ge(bt_out, HEADS)
                tile_mm(pe, a, 2 * a, tok=a >= 4, hbase=0 if a == 0 else None)
            diff_pe(pe)
            pe.wait_ge(y_lo, 8)
            for a in (6, 7):
                tile_mm(pe, a, 2 * a)
            stats_pe(pe, 1, 8)
            mlp_pe(pe, 0, 16)


        N_KV, N_C0, N_B0, N_C1, N_B1 = (HALF0[n] for n in ("kv", "cmp0", "b_in0", "cmp1", "b_in1"))
        kv_ev, f_ff, f_lo = sem("kv_ev"), sem("f_ff"), sem("f_lo")
        c_ev, c_sq, c_e, c_y = sem("c_ev"), sem("c_sq"), sem("c_e"), sem("c_y")
        c2_mm, kc_ev, vb_set, vb_ev = sem("c2_mm"), sem("kc_ev"), sem("vb_set"), sem("vb_ev")
        gw_hi, gw_lo, g_mm, g_e, g_ready = sem("gw_hi"), sem("gw_lo"), sem("g_mm"), sem("g_e"), sem("g_ready")
        kv2, kd, vB, gx, gt, gate = (sb[n] for n in ("kv2", "kd", "vB", "gx", "gt", "gate"))
        fH, fL, fF = sb["fH"], sb["fL"], sb["fF"]

        def spread(act, a, dst, shift):
            for m in range(4):
                o, freed = evac(act, a, m)
                s, g = m // 2, 2 * (m % 2)
                for j in range(2):
                    act.activation(dst[0:HD, s, g + j, :], o[j * HD:(j + 1) * HD, :], ACT.Copy).then_inc(kv_ev, 1)
                act.activation(dst[HD:P, s, g, 0:T - shift], o[0:HD, shift:T], ACT.Copy).then_inc(kv_ev, 1)
                act.activation(dst[HD:P, s, g + 1, 0:T - shift], o[HD:P, shift:T], ACT.Copy).then_inc(freed, 1)

        def flat_dve(dve, s):
            src = bass.AP(tensor=kv2[:, :, :, :].tensor, offset=kv2[:, s, 0, 0:1].offset,
                          ap=[kv2[:, :, :, :].ap[0], [2, 16], [T, GRP], [16, NCMP]])
            pos = sb["pos"][:, s, :].rearrange("p (l o q) -> p l o q", o=1, q=1).to_broadcast([P, 16, GRP, NCMP])
            for dst in (fH, fF):
                dve.tensor_tensor(dst[:, :, :].rearrange("p l (g n) -> p l g n", g=GRP), src, pos,
                                  ALU.add).then_inc(f_ff, 1)
            dve.wait_ge(f_ff, 2 * s + 2)
            dve.tensor_tensor(fL[:, :, :], fF[:, :, :], fH[:, :, :].bitcast(F32), ALU.subtract).then_inc(f_lo, 1)

        def cmp_pe(pe, s, n0):
            pe.wait_ge(f_lo, s + 1)
            if s == 0:
                pe.wait_ge(acc_free[0], 4 * 14)
            else:
                pe.wait_ge(c_ev, 2)
            for j in range(2):
                pe.wait_ge(w_lo, n0 + j + 1)
                for kk in range(8):
                    l = 8 * j + kk
                    for m in range(2):
                        last = three(pe, bank[:, m, 0:GRP * NCMP], wpart((n0 + j) % 2, kk, m * P, P, 256),
                                     (fH[:, l, :], fL[:, l, :]), l == 0, l == 15)
                last.then_inc(half_used, 1)

        def gelu_act(act, s, n):
            act.wait_ge(half_used, n)
            act.wait_ge(vb_set, 1)
            for m in range(2):
                act.activation(gx[:, s, m, :].rearrange("p (g n) -> p g n", g=GRP)[:, :, 0:NCMP],
                               bank[:, m, 0:GRP * NCMP].rearrange("p (g n) -> p g n", g=GRP),
                               ACT.Copy).then_inc(c_ev, 1)
            act.wait_ge(c_sq, 4 * s + 4)
            act.activation(gt[:, :, :], gt[:, :, :], ACT.Exp).then_inc(c_e, 1)

        def gelu_dve(dve, s):
            g = gx[:, s, :, :]
            dve.wait_ge(c_ev, 2 * s + 2)
            dve.tensor_tensor(gt[:, :, :], g, g, ALU.mult).then_inc(c_sq, 1)
            dve.wait_ge(c_sq, 4 * s + 1)
            dve.tensor_scalar(gt[:, :, :], gt[:, :, :], 0.044715, 1.0, ALU.mult, ALU.add).then_inc(c_sq, 1)
            dve.wait_ge(c_sq, 4 * s + 2)
            dve.tensor_tensor(gt[:, :, :], gt[:, :, :], g, ALU.mult).then_inc(c_sq, 1)
            dve.wait_ge(c_sq, 4 * s + 3)
            dve.tensor_scalar(gt[:, :, :], gt[:, :, :], -2.0 * math.sqrt(2.0 / math.pi), 80.0, ALU.mult,
                              ALU.min).then_inc(c_sq, 1)
            dve.wait_ge(c_e, s + 1)
            dve.tensor_scalar(gt[:, :, :], gt[:, :, :], 1.0, None, ALU.add).then_inc(c_y, 1)
            dve.wait_ge(c_y, 3 * s + 1)
            dve.reciprocal(gt[:, :, :], gt[:, :, :]).then_inc(c_y, 1)
            dve.wait_ge(c_y, 3 * s + 2)
            dve.tensor_tensor(g, g, gt[:, :, :], ALU.mult).then_inc(c_y, 1)

        def cmp2_pe(pe):
            pe.wait_ge(c_y, 8)
            pe.wait_ge(acc_free[1], 4 * 14)
            for m in range(2):
                last = pe.matmul(bank[:, 4, 0:P], sb["cw2"][:, 0, m, :], gx[:, 0, m, :], start=m == 0, stop=m == 1)
            last.then_inc(c2_mm, 1)
            for g in range(GRP):
                for m in range(2):
                    last = pe.matmul(bank[:, 5, g * HD:(g + 1) * HD], sb["yr"][:, m, g, :], sb["cw2"][:, 1, m, 0:HD],
                                     start=m == 0, stop=m == 1)
            last.then_inc(c2_mm, 1)

        UNITS = []
        for i in range(NT):
            for g in range(GRP):
                if i == 0:
                    split = [[(b, r) for b in range(2) for r in (e, e + 2)] for e in range(2)]
                elif i == 1:
                    split = [[(b, e), (b, e + 2)] for b in range(2) for e in range(2)]
                else:
                    split = [[(b, r)] for b in range(2) for r in range(4)]
                UNITS += [(i, g, (i + 1) * P, heads) for heads in split]
        UN = len(UNITS)
        SCORED = [sum(len(x[3]) for x in UNITS[:u + 1]) for u in range(UN)]
        OF_BRANCH = {(x[0], x[1], b): u for u, x in enumerate(UNITS) for b, r in x[3]}
        FIRST = [next(u for u in range(UN) if UNITS[u][0] == i) for i in range(NT)] + [UN]
        n_mm, n_max, n_exp, n_t, n_pt, n_pv = (sem(n) for n in ("n_mm", "n_max", "n_exp", "n_t", "n_pt", "n_pv"))
        n_w, n_o, n_sum = sem("n_w"), sem("n_o"), sem("n_sum")
        x_mm, x_s, x_m, x_sub, x_exp, x_sum, x_w, x_t, x_pt = (sem(n) for n in (
            "x_mm", "x_s", "x_m", "x_sub", "x_exp", "x_sum", "x_w", "x_t", "x_pt"))
        sB, pB, ptB, oB, sc, ptc, cx, wr, cmask = (sb[n] for n in (
            "sB", "pB", "ptB", "oB", "sc", "ptc", "cx", "wr", "cmask"))

        def parts(u):
            i, g, w, heads = UNITS[u]
            n0 = SCORED[u] - len(heads)
            return [(n0 + q, slice(q * w, (q + 1) * w), (((i * GRP + g) * 2 + b) * 4 + r) % 64, b, r)
                    for q, (b, r) in enumerate(heads)]

        def o_unit(i, g, b):
            return (i * GRP + g) * 3 + b

        def nsa_pe(pe):
            def scores(u):
                i, g, w, heads = UNITS[u]
                if u >= 2:
                    pe.wait_ge(n_max, SCORED[u - 2])
                for n, part, c, b, r in parts(u):
                    half = slice((r % 2) * HD, (r % 2 + 1) * HD)
                    last = pe.matmul(bank[:, u % 2, part], qT[half, (4 * g + r) // 2, i * P:(i + 1) * P],
                                     kd[half, b, g, 0:w], start=True, stop=True)
                last.then_inc(n_mm, 1)

            def turn(u):
                pe.wait_ge(n_exp, SCORED[u])
                if u >= 2:
                    pe.wait_ge(n_pt, u - 1)
                for j in range(len(UNITS[u][3]) * UNITS[u][2] // P):
                    last = pe.transpose(bank[:, 2 + u % 2, j * P:(j + 1) * P], pB[:, u % 2, j * P:(j + 1) * P],
                                        ident[:, :])
                last.then_inc(n_t, 1)

            opened = [0]

            def o_bank(ou):
                if ou >= 2 and ou == opened[0]:
                    pe.wait_ge(n_o, ou - 1)
                opened[0] = max(opened[0], ou + 1)
                return bank[:, 4 + ou % 2, :]

            def compressed(i, g):
                if g == 0:
                    pe.wait_ge(x_pt, i + 1)
                    pe.wait_ge(vb_ev, 4)
                pe.matmul(o_bank(o_unit(i, g, 0))[:, 0:256], ptc[:, g * P:(g + 1) * P], sb["vblk"][:, g, :],
                          start=True, stop=True).then_inc(n_pv, 1)

            def values(u):
                i, g, w, heads = UNITS[u]
                if u == FIRST[i] + g * (FIRST[i + 1] - FIRST[i]) // GRP:
                    compressed(i, g)
                pe.wait_ge(n_pt, u + 1)
                for q, (n, part, c, b, r) in enumerate(parts(u)):
                    o = o_bank(o_unit(i, g, b + 1))
                    for j in range(i + 1):
                        last = pe.matmul(o[:, r * HD:(r + 1) * HD],
                                         ptB[:, u % 2, part.start + j * P:part.start + (j + 1) * P],
                                         vB[:, j, b * 256 + g * HD:b * 256 + (g + 1) * HD], start=j == 0, stop=j == i)
                    if OF_BRANCH[i, g, b] == u and (q + 1 == len(heads) or heads[q + 1][0] != b):
                        last.then_inc(n_pv, 1)

            def c_scores(i):
                if i == 0:
                    pe.wait_ge(kc_ev, 1)
                else:
                    pe.wait_ge(x_pt, i)
                if i >= 2:
                    pe.wait_ge(y_lo, 8 + 2 * (i - 1))
                for hd in range(HEADS):
                    lo_, hi_ = (hd % 2) * HD, (hd % 2 + 1) * HD
                    last = pe.matmul(bank[:, 6 + hd % 2, (hd // 2) * 32:(hd // 2 + 1) * 32],
                                     qT[lo_:hi_, hd // 2, i * P:(i + 1) * P],
                                     sb["kcd"][lo_:hi_, (hd // 4) * 32:(hd // 4 + 1) * 32], start=True, stop=True)
                    if hd >= HEADS - 2:
                        last.then_inc(x_mm, 1)

            def c_turn(i):
                pe.wait_ge(x_w, 3 * (i + 1))
                for g in range(GRP):
                    last = pe.transpose(bank[:, 6, g * P:(g + 1) * P],
                                        sc[:, 4 * g:4 * g + 4, :].rearrange("p a b -> p (a b)"), ident[:, :])
                last.then_inc(x_t, 1)

            def tail(i):
                pe.wait_ge(n_o, 12 * (i + 1))
                if i + 1 < NT:
                    pe.wait_ge(x_pt, i + 2)
                for r in range(2):
                    for h in range(4):
                        last = pe.transpose(bank[:, 6 + r, h * P:(h + 1) * P],
                                            oB[:, i % 2, 2 * r + h // 2, (h % 2) * P:(h % 2 + 1) * P], ident[:, :])
                    last.then_inc(y_t, 1)

            for u in range(-6, UN + 5):
                for i in range(NT):
                    if u == FIRST[i] - 6:
                        c_scores(i)
                if 0 <= u + 2 < UN:
                    scores(u + 2)
                if 0 <= u - 2 < UN:
                    values(u - 2)
                if 0 <= u < UN:
                    turn(u)
                for i in range(NT):
                    if u == FIRST[i] - 2:
                        c_turn(i)
                    if u == FIRST[i + 1] + 4:
                        tail(i)

        def nsa_dve(dve):
            def bias_max(u):
                i, g, w, heads = UNITS[u]
                dve.wait_ge(n_mm, u + 1)
                if u >= 2:
                    dve.wait_ge(n_exp, SCORED[u - 2])
                for n, part, c, b, r in parts(u):
                    dve.tensor_tensor_reduce(sB[:, u % 2, part], bank[:, u % 2, part], sb["bt"][:, 4 * g + r, T - w:T],
                                             -SCALE, BIG, ALU.add, ALU.min, nm[:, c:c + 1]).then_inc(n_max, 1)

            def spread4(a):
                return a.rearrange("p (h o) -> p h o", o=1).to_broadcast([P, 4, HD])

            def out_unit(i, g, b):
                ou = o_unit(i, g, b)
                k = 2 * (i * GRP + g) + b - 1
                if b > 0:
                    c = wr[:, k % 4, :]
                    u0 = (4 * k) % 64
                    dve.wait_ge(n_exp, SCORED[OF_BRANCH[i, g, b - 1]])
                    dve.reciprocal(c, rs[:, u0:u0 + 4]).then_inc(n_w, 1)
                    dve.wait_ge(n_w, 2 * k + 1)
                    dve.tensor_tensor(c, c, gate[:, i, 4 * g:4 * g + 4, b], ALU.mult).then_inc(n_w, 1)
                    dve.wait_ge(n_w, 2 * k + 2)
                else:
                    c = cx[:, 2 + i % 2, 4 * g:4 * g + 4]
                    dve.wait_ge(x_w, 3 * (i + 1))
                dve.wait_ge(n_pv, ou + 1)
                p = bank[:, 4 + ou % 2, 0:256].rearrange("p (h d) -> p h d", h=4)
                o = oB[:, i % 2, g, :].rearrange("p (h d) -> p h d", h=4)
                if b == 0:
                    if i >= 2 and g == 0:
                        dve.wait_ge(y_t, 8 + 2 * (i - 1))
                    dve.tensor_tensor(o, p, spread4(c), ALU.mult).then_inc(n_o, 1)
                    return
                t = tmp3
                dve.tensor_tensor(t, p, spread4(c), ALU.mult).then_inc(n_sum, 1)
                dve.wait_ge(n_sum, k + 1)
                dve.wait_ge(n_o, ou)
                dve.tensor_tensor(o, o, t, ALU.add).then_inc(n_o, 1)

            tmp3 = sb["ot"][:, :].rearrange("p (h d) -> p h d", h=4)

            def c_mask(i):
                dve.wait_ge(x_mm, 2 * (i + 1))
                if i >= 1:
                    dve.wait_ge(x_t, i)
                s2 = sc[:, :, :].rearrange("p (h e) n -> p e h n", e=2)
                for e in range(2):
                    dve.scalar_tensor_tensor(
                        out=s2[:, e], in0=bank[:, 6 + e, 0:256].rearrange("p (h n) -> p h n", n=32), scalar=SCALE,
                        in1=cmask[:, i, 0:32].rearrange("p (o n) -> p o n", o=1).to_broadcast([P, 8, 32]),
                        op0=ALU.mult, op1=ALU.add).then_inc(x_s, 1)
                dve.wait_ge(x_s, 2 * (i + 1))
                dve.tensor_reduce(cx[:, 0, :], sc[:, :, :], AX.X, ALU.max).then_inc(x_m, 1)
                dve.wait_ge(x_m, i + 1)
                dve.tensor_tensor(sc[:, :, :], sc[:, :, :],
                                  cx[:, 0, :].rearrange("p (h o) -> p h o", o=1).to_broadcast([P, HEADS, 32]),
                                  ALU.subtract).then_inc(x_sub, 1)

            def c_norm(i):
                dve.wait_ge(x_exp, i + 1)
                dve.tensor_reduce(cx[:, 1, :], sc[:, :, :], AX.X, ALU.add).then_inc(x_sum, 1)
                dve.wait_ge(x_sum, i + 1)
                dve.tensor_tensor(sc[:, :, :], sc[:, :, :],
                                  cmask[:, i, 32:64].rearrange("p (o n) -> p o n", o=1).to_broadcast([P, HEADS, 32]),
                                  ALU.mult).then_inc(x_w, 1)
                c = cx[:, 2 + i % 2, :]
                dve.reciprocal(c, cx[:, 1, :]).then_inc(x_w, 1)
                dve.wait_ge(x_w, 3 * i + 2)
                dve.tensor_tensor(c, c, gate[:, i, :, 0], ALU.mult).then_inc(x_w, 1)

            def tail(i):
                for r in range(2):
                    dve.wait_ge(y_hi, 8 + 2 * i + r + 1)
                    dve.tensor_tensor(hL[:, 4 * r:4 * r + 4, i * P:(i + 1) * P],
                                      bank[:, 6 + r, :].rearrange("p (h q) -> p h q", h=4),
                                      hH[:, 4 * r:4 * r + 4, i * P:(i + 1) * P].bitcast(F32),
                                      ALU.subtract).then_inc(y_lo, 1)

            for u in range(-6, UN + 6):
                for i in range(NT):
                    if u == FIRST[i] - 5:
                        c_mask(i)
                    if u == FIRST[i] - 3:
                        c_norm(i)
                if 0 <= u - 3 < UN:
                    i, g, w, heads = UNITS[u - 3]
                    if u - 3 == FIRST[i] + g * (FIRST[i + 1] - FIRST[i]) // GRP:
                        out_unit(i, g, 0)
                    for b in range(2):
                        if OF_BRANCH[i, g, b] == u - 3:
                            out_unit(i, g, b + 1)
                if 0 <= u + 2 < UN:
                    bias_max(u + 2)
                for i in range(NT):
                    if u == FIRST[i + 1] + 5:
                        tail(i)

        def nsa_act(act):
            def exps(u):
                if u >= 2:
                    act.wait_ge(n_t, u - 1)
                for n, part, c, b, r in parts(u):
                    act.wait_ge(n_max, n + 1)
                    act.activation(pB[:, u % 2, part], sB[:, u % 2, part], ACT.Exp, bias=nm[:, c:c + 1], scale=-1.0,
                                   accum_out=rs[:, c:c + 1]).then_inc(n_exp, 1)

            def copy_out(u):
                w = len(UNITS[u][3]) * UNITS[u][2]
                act.wait_ge(n_t, u + 1)
                act.activation(ptB[:, u % 2, 0:w], bank[:, 2 + u % 2, 0:w], ACT.Copy).then_inc(n_pt, 1)

            def c_exp(i):
                act.wait_ge(x_sub, i + 1)
                act.activation(sc[:, :, :], sc[:, :, :], ACT.Exp).then_inc(x_exp, 1)

            def c_copy(i):
                act.wait_ge(x_t, i + 1)
                if i >= 1:
                    act.wait_ge(n_pv, o_unit(i - 1, 3, 0) + 1)
                act.activation(ptc[:, :], bank[:, 6, :], ACT.Copy).then_inc(x_pt, 1)

            def tail(i):
                for r in range(2):
                    act.wait_ge(y_t, 8 + 2 * i + r + 1)
                    act.activation(hH[:, 4 * r:4 * r + 4, i * P:(i + 1) * P],
                                   bank[:, 6 + r, :].rearrange("p (h q) -> p h q", h=4), ACT.Copy).then_inc(y_hi, 1)

            for u in range(-6, UN + 6):
                for i in range(NT):
                    if u == FIRST[i] - 4:
                        c_exp(i)
                if 0 <= u + 1 < UN:
                    exps(u + 1)
                if 0 <= u < UN:
                    copy_out(u)
                for i in range(NT):
                    if u == FIRST[i]:
                        c_copy(i)
                    if u == FIRST[i + 1] + 5:
                        tail(i)

        def sp_second(sp):
            for n in range(N_KV + 2, HALF0["mlp1"] + 2):
                if n == HALF0["b_out"] + 2:
                    sp.wait_ge(y_lo, 8 + 8)
                    for name in ("gm", "mmask"):
                        sp.dma_start(sb[name].ap(), d[name]).then_inc(par3_in, 16)
                load_half(sp, n)
            mlp_sp(sp, 1)

        def act_second(act):
            stats_act(act, 2, xw_evac(22), 24)
            act.wait_ge(mod_ready, 8)
            apply_act(act, 2, lambda c: mod(104 + c), lambda c: mod(96 + c))
            for a in (24, 25, 26):
                n = N_KV + 2 * (a - 24)
                hi(act, n + 2)
                hi(act, n + 3)
                act.wait_ge(half_used, n + 2)
                if a < 26:
                    spread(act, a, kv2 if a == 24 else kd, 1 if a == 24 else 0)
                else:
                    for m in range(4):
                        o, freed = evac(act, a, m)
                        act.activation(vB[:, m, :], o, ACT.Copy).then_inc(freed, 1)
            apply_act(act, 3, lambda c: mod(56 + c), lambda c: mod(48 + c))
            hi(act, N_B0)
            hi(act, N_B0 + 1)
            gelu_act(act, 0, N_B0)
            hi(act, N_C1)
            hi(act, N_C1 + 1)
            for a, n in ((27, N_B0), (28, N_B1)):
                act.wait_ge(half_used, n + 2)
                for m in range(4):
                    o, freed = evac(act, a, m)
                    act.activation(qT[:, 4 * (a - 27) + m, :], o, ACT.Copy).then_inc(freed, 1)
                if a == 27:
                    hi(act, N_B1)
                    hi(act, N_B1 + 1)
                    gelu_act(act, 1, N_B1)
                    hi(act, HALF0["b_out"])
                    act.wait_ge(f_ff, 4)
                    act.wait_ge(half_used, N_B1)
                    act.activation(sb["gwH"][:, :, :], sb["gw"][:, :, :], ACT.Copy).then_inc(gw_hi, 1)
            hi(act, HALF0["b_out"] + 1)
            act.wait_ge(c2_mm, 1)
            act.activation(sb["kcd"][:, :], bank[:, 4, 0:P], ACT.Copy).then_inc(kc_ev, 1)
            act.wait_ge(g_mm, 1)
            act.activation(gate[:, :, :, :].rearrange("p t h b -> p t (h b)"),
                           bank[:, 6, 0:NT * 48].rearrange("p (t n) -> p t n", t=NT), ACT.Exp, scale=-1.0)\
                .then_inc(g_e, 1)
            nsa_act(act)
            for a in (29, 30):
                n = HALF0["b_out"] + 2 * (a - 29)
                hi(act, n + 2)
                hi(act, n + 3)
            stats_act(act, 3, xw_evac(29), 31)
            apply_act(act, 4, lambda c: mod(80 + c), lambda c: mod(72 + c))
            mlp_act(act, 1)
            stats_act(act, 4, xw_evac(45), 47)

        def dve_second(dve):
            dve.wait_ge(mst, 5)
            mod_scale(dve, 104, ("kv_norm", 0))
            mod_scale(dve, 56, ("attn_norm", 8))
            mod_scale(dve, 80, ("mlp_norm", 8))
            apply_dve(dve, 2, 2)
            for n in range(N_KV + 2, N_KV + 8):
                lo(dve, n)
            dve.memset(gx[:, :, :, :], 0.0).then_inc(vb_set, 1)
            dve.wait_ge(par2_in, 64)
            for j in range(2):
                dve.wait_ge(ada_in[j], 16 * (ADA_ALL - ADA_FIRST) // 2)
            dve.wait_ge(acc_free[0], 4 * 13)
            flat_dve(dve, 0)
            apply_dve(dve, 3, 2)
            lo(dve, N_B0)
            lo(dve, N_B0 + 1)
            dve.wait_ge(half_used, N_B0)
            flat_dve(dve, 1)
            gelu_dve(dve, 0)
            lo(dve, N_C1)
            lo(dve, N_C1 + 1)
            lo(dve, N_B1)
            lo(dve, N_B1 + 1)
            gelu_dve(dve, 1)
            dve.wait_ge(c_y, 6)
            for m in range(2):
                dve.tensor_copy(sb["yr"][:, m, :, :].rearrange("p g (r n) -> p g r n", r=4),
                                gx[:, 1, m, :].rearrange("p (g o n) -> p g o n", g=GRP, o=1)
                                .to_broadcast([P, GRP, 4, 32])).then_inc(c_y, 1)
            lo(dve, HALF0["b_out"])
            dve.wait_ge(gw_hi, 1)
            dve.tensor_tensor(sb["gwL"][:, :, :], sb["gw"][:, :, :], sb["gwH"][:, :, :].bitcast(F32),
                              ALU.subtract).then_inc(gw_lo, 1)
            lo(dve, HALF0["b_out"] + 1)
            dve.wait_ge(c2_mm, 2)
            dve.memset(sb["vblk"][:, :, :], 0.0).then_inc(vb_set, 1)
            dve.wait_ge(vb_set, 2)
            for r in range(4):
                dve.tensor_copy(sb["vblk"][32 * r:32 * r + 32, :, r * HD:(r + 1) * HD],
                                bank[32 * r:32 * r + 32, 5, 0:256].rearrange("p (g d) -> p g d", g=GRP))\
                    .then_inc(vb_ev, 1)
            dve.wait_ge(g_e, 1)
            dve.tensor_scalar(gate[:, :, :, :], gate[:, :, :, :], 1.0, None, ALU.add).then_inc(g_ready, 1)
            dve.wait_ge(g_ready, 1)
            dve.reciprocal(gate[:, :, :, :], gate[:, :, :, :]).then_inc(g_ready, 1)
            dve.wait_ge(g_ready, 2)
            nsa_dve(dve)
            for a in (29, 30):
                n = HALF0["b_out"] + 2 * (a - 29)
                lo(dve, n + 2)
                lo(dve, n + 3)
                dve.wait_ge(half_used, n + 2)
                residual_dve(dve, a, 4 * (a - 29), lambda c: mod(64 + c))
            apply_dve(dve, 4, 3)
            mlp_dve(dve, 1)
            dve.wait_ge(rstd_done, 5)
            for c in range(KC):
                dve.scalar_tensor_tensor(out=x[:, c, :], in0=x[:, c, :], scalar=col("final_norm", c), in1=rstd[:, :],
                                         op0=ALU.mult, op1=ALU.mult).then_inc(f_norm, 1)

        f_norm, par3_in = sem("f_norm"), sem("par3_in")

        def pe_second(pe):
            stats_pe(pe, 2, 24)
            for a in (24, 25, 26):
                tile_mm(pe, a, N_KV + 2 * (a - 24), tok=a == 26, hbase=16 if a == 24 else None)
            cmp_pe(pe, 0, N_C0)
            tile_mm(pe, 27, N_B0, hbase=24)
            cmp_pe(pe, 1, N_C1)
            pe.wait_ge(c_ev, 4)
            tile_mm(pe, 28, N_B1)
            cmp2_pe(pe)
            pe.wait_ge(gw_lo, 1)
            for m in range(NT):
                for k in range(KC):
                    last = three(pe, bank[:, 6, m * 48:(m + 1) * 48],
                                 (hH[:, k, m * P:(m + 1) * P], hL[:, k, m * P:(m + 1) * P]),
                                 (sb["gwH"][:, k, :], sb["gwL"][:, k, :]), k == 0, k == KC - 1)
            last.then_inc(g_mm, 1)
            pe.wait_ge(g_e, 1)
            pe.wait_ge(acc_free[0], 4 * 15)
            nsa_pe(pe)
            pe.wait_ge(y_lo, 8 + 8)
            for a in (29, 30):
                tile_mm(pe, a, HALF0["b_out"] + 2 * (a - 29))
            stats_pe(pe, 3, 31)
            mlp_pe(pe, 1, 40)
            stats_pe(pe, 4, 47)

        N_MI, N_MO, N_G0, N_P0 = (HALF0[n] for n in ("m_in", "m_out", "ple0g", "ple0p"))
        gm_hi, gm_lo, gg_mm = sem("gm_hi"), sem("gm_lo"), sem("gg_mm")
        r_act, r_dve, rc_mm, rb_mm, rc_ev, rb_ev = (sem(n) for n in ("r_act", "r_dve", "rc_mm", "rb_mm", "rc_ev", "rb_ev"))
        cv, cv_e, cv_y, xc0 = sem("cv"), sem("cv_e"), sem("cv_y"), sem("xc0")
        og, zz_e, zz = sem("og"), sem("zz_e"), sem("zz")
        l_s, l_nd, l_e, l_w, l_o, l_d, l_h, l_q, l_r, l_y, l_t = (sem(n) for n in (
            "l_s", "l_nd", "l_e", "l_w", "l_o", "l_d", "l_h", "l_q", "l_r", "l_y", "l_t"))
        qkM, xc, rows, wt, vM, oM, zM, negM, negD, yM = (sb[n] for n in (
            "qkM", "xc", "rows", "wt", "vM", "oM", "zM", "negM", "negD", "yM"))
        aC, eC = nm[:, 0:16].rearrange("p (t h) -> p t h", h=4), nm[:, 16:32].rearrange("p (t h) -> p t h", h=4)
        M_H = 4
        MK = P ** -0.5

        def m_gates_pe(pe):
            pe.wait_ge(gm_lo, 1)
            acc_wait(pe, 50)
            for k in range(KC):
                last = three(pe, bank[:, 0, :], (sb["gmH"][:, k, :], sb["gmL"][:, k, :]), (hH[:, k, :], hL[:, k, :]),
                             k == 0, k == KC - 1)
            last.then_inc(gg_mm, 1)

        def m_gates_act(act):
            act.wait_ge(gg_mm, 1)
            act.wait_ge(r_dve, 1)
            act.activation(rows[:, 0, :], bank[0:4, 0, :], ACT.Identity, bias=cols[0:4, COL0["b_gate"]:COL0["b_gate"] + 1])\
                .then_inc(r_act, 1)
            act.activation(rows[:, 1, :], bank[32:36, 0, :], ACT.Identity,
                           bias=cols[0:4, COL0["b_gate"] + 1:COL0["b_gate"] + 2]).then_inc(r_act, 1)
            act.wait_ge(r_dve, 3)
            act.activation(rows[:, 2, :], rows[:, 2, :], ACT.Exp).then_inc(r_act, 1)
            act.wait_ge(r_act, 3)
            act.activation(rows[:, 2, :], rows[:, 2, :], ACT.Ln, bias=sb["ones"][0:4, :]).then_inc(r_act, 1)
            act.wait_ge(r_dve, 8)
            act.activation(rows[:, 3, :], rows[:, 3, :], ACT.Exp, scale=-1.0).then_inc(r_act, 1)

        def m_gates_dve(dve):
            r = [rows[:, j, :] for j in range(4)]
            dve.memset(r[3], 0.0).then_inc(r_dve, 1)
            dve.wait_ge(r_act, 2)
            dve.tensor_scalar(r[2], r[1], -1.0, None, ALU.mult).then_inc(r_dve, 1)
            dve.wait_ge(r_dve, 2)
            dve.tensor_tensor(r[2], r[2], r[1], ALU.min).then_inc(r_dve, 1)
            dve.wait_ge(r_act, 4)
            dve.scalar_tensor_tensor(out=r[1], in0=r[1], scalar=0.0, in1=r[2], op0=ALU.min, op1=ALU.subtract)\
                .then_inc(r_dve, 1)
            dve.wait_ge(r_dve, 4)
            dve.tensor_tensor_scan(r[1], r[1], r[3], 0.0, ALU.add, ALU.add).then_inc(r_dve, 1)
            dve.wait_ge(r_dve, 5)
            dve.tensor_tensor(r[0], r[0], r[1], ALU.subtract).then_inc(r_dve, 1)
            dve.wait_ge(r_dve, 6)
            dve.tensor_tensor_scan(r[2], r[0], r[0], 0.0, ALU.max, ALU.max).then_inc(r_dve, 1)
            dve.wait_ge(r_dve, 7)
            dve.tensor_tensor(r[3], r[1], r[2], ALU.add).then_inc(r_dve, 1)

        def m_rows_pe(pe):
            pe.wait_ge(r_act, 5)
            for i in range(NT):
                for q, j in enumerate((0, 3)):
                    last = pe.transpose(bank[:, 1, (4 * q + i) * 4:(4 * q + i) * 4 + 4], rows[:, j, i * P:(i + 1) * P],
                                        ident[0:4, 0:4])
            last.then_inc(rc_mm, 1)
            for h in range(M_H):
                if h >= 2:
                    pe.wait_ge(rb_ev, h - 1)
                pe.matmul(bank[:, 2 + h % 2, :], ident[0:4, h:h + 1].to_broadcast([4, P]), rows[:, 2, :],
                          start=True, stop=True).then_inc(rb_mm, 1)

        def m_rows_act(act):
            act.wait_ge(rc_mm, 1)
            act.activation(nm[:, 0:32], bank[:, 1, 0:32], ACT.Copy).then_inc(rc_ev, 1)
            act.wait_ge(gg_mm, 1)
            for h in range(M_H):
                act.wait_ge(rb_mm, h + 1)
                act.activation(negM[:, h, :], bank[:, 2 + h % 2, :], ACT.Copy, scale=-1.0).then_inc(rb_ev, 1)

        def conv_act(act, a):
            for m in range(4):
                c = 4 * (a - 47) + m
                if c == 0:
                    act.wait_ge(xc0, 2)
                if c >= 2:
                    act.wait_ge(cv, 4 * (c - 1))
                o, freed = evac(act, a, m)
                act.activation(xc[:, c % 2, 3:T + 3], o, ACT.Copy).then_inc(freed, 1)
                if c >= 1:
                    conv_exp(act, c - 1)
            if a == 48:
                conv_exp(act, 7)

        def conv_exp(act, c):
            act.wait_ge(cv, 4 * (c + 1))
            if c >= 3:
                act.wait_ge(cv_y, 3 * (c - 2))
            act.activation(tmp[:, c % 3, :], qkM[:, c, :], ACT.Exp, scale=-1.0).then_inc(cv_e, 1)

        def conv_dve(dve, a):
            for m in range(4):
                c = 4 * (a - 47) + m
                dve.wait_ge(acc_free[a % 2], 4 * (a // 2) + m + 1)
                y = qkM[:, c, :]
                for n, j in enumerate((3, 2, 1, 0)):
                    tap = col("conv", 8 * j + c)
                    src = xc[:, c % 2, j:j + T]
                    if n == 0:
                        dve.tensor_scalar(y, src, tap, None, ALU.mult).then_inc(cv, 1)
                    else:
                        dve.wait_ge(cv, 4 * c + n)
                        dve.scalar_tensor_tensor(out=y, in0=src, scalar=tap, in1=y, op0=ALU.mult, op1=ALU.add)\
                            .then_inc(cv, 1)
                if c >= 1:
                    conv_silu(dve, c - 1)
            if a == 48:
                conv_silu(dve, 7)

        def conv_silu(dve, c):
            e = tmp[:, c % 3, :]
            dve.wait_ge(cv_e, c + 1)
            dve.tensor_scalar(e, e, 1.0, None, ALU.add).then_inc(cv_y, 1)
            dve.wait_ge(cv_y, 3 * c + 1)
            dve.reciprocal(e, e).then_inc(cv_y, 1)
            dve.wait_ge(cv_y, 3 * c + 2)
            dve.scalar_tensor_tensor(out=qkM[:, c, :], in0=qkM[:, c, :], scalar=1.0 if c < 4 else MK, in1=e,
                                     op0=ALU.mult, op1=ALU.mult).then_inc(cv_y, 1)

        def m_core_pe(pe):
            pe.wait_ge(cv_y, 24)
            pe.wait_ge(rb_ev, 4)
            pe.wait_ge(acc_free[0], 4 * 28)
            pe.wait_ge(acc_free[1], 4 * 27)
            for h in range(M_H + 2):
                if h < M_H:
                    for j in range(NT):
                        u = 4 * h + j
                        if u >= 2:
                            pe.wait_ge(l_w, u - 1)
                        pe.matmul(bank[:, u % 2, j * P:T], qkM[:, 4 + h, j * P:(j + 1) * P], qkM[:, h, j * P:T],
                                  start=True, stop=True).then_inc(l_s, 1)
                if 1 <= h <= M_H:
                    g = h - 1
                    pe.wait_ge(l_w, 4 * g + 4)
                    for i in range(NT):
                        v = 4 * g + i
                        if v >= 2:
                            pe.wait_ge(l_h, v - 1)
                        for part in range(2):
                            for j in range(i + 1):
                                rhs = vM[:, j, g * 256:(g + 1) * 256] if part == 0 else sb["ones"][:, 0:1]
                                o = bank[:, 2 + v % 2, 0:256] if part == 0 else bank[:, 2 + v % 2, 256:257]
                                last = pe.matmul(o, wt[:, g % 2, j, i * P:(i + 1) * P], rhs, start=j == 0, stop=j == i)
                        last.then_inc(l_o, 1)
                if h >= 2:
                    g = h - 2
                    pe.wait_ge(l_y, 4 * g + 4)
                    for e in range(2):
                        if g >= 1:
                            pe.wait_ge(y_lo, 16 + 2 * (g - 1) + e + 1)
                        for i in range(NT):
                            last = pe.transpose(bank[:, 4 + e, i * P:(i + 1) * P], yM[:, g % 2, i, e * P:(e + 1) * P],
                                                ident[:, :])
                        last.then_inc(l_t, 1)

        def m_core_act(act):
            for h in range(M_H + 2):
                if h < M_H:
                    act.wait_ge(l_nd, h + 1)
                    act.wait_ge(rc_ev, 1)
                    if h >= 2:
                        act.wait_ge(l_o, 4 * (h - 1))
                    for j in range(NT):
                        act.activation(wt[:, h % 2, j, j * P:(j + 1) * P], negD[:, h, j, :], ACT.Exp,
                                       bias=aC[:, j, h:h + 1]).then_inc(l_e, 1)
                        if j + 1 < NT:
                            act.activation(wt[:, h % 2, j, (j + 1) * P:T], negM[:, h, (j + 1) * P:T], ACT.Exp,
                                           bias=aC[:, j, h:h + 1]).then_inc(l_e, 1)
                if 1 <= h <= M_H:
                    g = h - 1
                    for i in range(NT):
                        v = 4 * g + i
                        act.wait_ge(l_h, v + 1)
                        act.activation(negD[:, g, 0:2, :].rearrange("p a b -> p (a b)"), yM[:, g % 2, i, :], ACT.Square,
                                       accum_out=ssq[:, v:v + 1]).then_inc(l_q, 1)
                        act.wait_ge(l_q, v + 1)
                    r = ssq[:, 4 * g:4 * g + 4]
                    act.activation(r, r, ACT.Ln, bias=one[:, 1:2], scale=1.0 / 256).then_inc(l_r, 1)
                    act.wait_ge(l_r, 2 * g + 1)
                    act.activation(r, r, ACT.Exp, scale=-0.5).then_inc(l_r, 1)
                if h >= 2:
                    g = h - 2
                    for e in range(2):
                        act.wait_ge(l_t, 2 * g + e + 1)
                        act.activation(hH[:, 2 * g + e, :], bank[:, 4 + e, :], ACT.Copy,
                                       scale=col("hnorm", 2 * g + e)).then_inc(y_hi, 1)

        def m_core_dve(dve):
            dve.wait_ge(par3_in, 32)
            for h in range(M_H):
                dve.wait_ge(rb_ev, h + 1)
                dve.tensor_tensor(negD[:, h, :, :], negM[:, h, :].rearrange("p (t q) -> p t q", t=NT),
                                  sb["mmask"][:, :].rearrange("p (o q) -> p o q", o=1).to_broadcast([P, NT, P]),
                                  ALU.add).then_inc(l_nd, 1)
            for h in range(M_H + 2):
                if h < M_H:
                    for j in range(NT):
                        u = 4 * h + j
                        dve.wait_ge(l_s, u + 1)
                        dve.wait_ge(l_e, 7 * h + min(2 * j + 2, 7))
                        w = wt[:, h % 2, j, j * P:T]
                        dve.tensor_tensor(w, bank[:, u % 2, j * P:T], w, ALU.mult).then_inc(l_w, 1)
                if 1 <= h <= M_H:
                    g = h - 1
                    for i in range(NT):
                        v = 4 * g + i
                        dve.wait_ge(l_o, v + 1)
                        c = rs[:, v:v + 1]
                        den = bank[:, 2 + v % 2, 256:257]
                        dve.scalar_tensor_tensor(out=c, in0=den, scalar=-1.0, in1=eC[:, i, g:g + 1], op0=ALU.mult,
                                                 op1=ALU.max).then_inc(l_d, 1)
                        dve.wait_ge(l_d, 3 * v + 1)
                        dve.tensor_tensor(c, den, c, ALU.max).then_inc(l_d, 1)
                        dve.wait_ge(l_d, 3 * v + 2)
                        dve.reciprocal(c, c).then_inc(l_d, 1)
                        dve.wait_ge(l_d, 3 * v + 3)
                        if g >= 2 and i == 0:
                            dve.wait_ge(l_t, 2 * (g - 1))
                        dve.scalar_tensor_tensor(out=yM[:, g % 2, i, :], in0=bank[:, 2 + v % 2, 0:256], scalar=c,
                                                 in1=oM[:, i, g * 256:(g + 1) * 256], op0=ALU.mult, op1=ALU.mult)\
                            .then_inc(l_h, 1)
                    dve.wait_ge(l_r, 2 * g + 2)
                    for i in range(NT):
                        v = 4 * g + i
                        dve.scalar_tensor_tensor(out=yM[:, g % 2, i, :], in0=yM[:, g % 2, i, :], scalar=ssq[:, v:v + 1],
                                                 in1=zM[:, i, g * 256:(g + 1) * 256], op0=ALU.mult, op1=ALU.mult)\
                            .then_inc(l_y, 1)
                if h >= 2:
                    g = h - 2
                    for e in range(2):
                        c = 2 * g + e
                        dve.wait_ge(y_hi, 16 + c + 1)
                        dve.scalar_tensor_tensor(out=hL[:, c, :], in0=bank[:, 4 + e, :], scalar=col("hnorm", c),
                                                 in1=hH[:, c, :].bitcast(F32), op0=ALU.mult, op1=ALU.subtract)\
                            .then_inc(y_lo, 1)

        ple_s, p_in, p_hi, p_lo, ple_x = (sem(n) for n in (
            "ple_s", "p_in", "p_hi", "p_lo", "ple_x"))
        sg, pF, pH, pL = sb["sg"], sb["pF"], sb["pH"], sb["pL"]

        def ple_act(act, l, a, n):
            act.wait_ge(p_in, 16 * (l + 1))
            act.activation(pH[:, :, :], pF[:, :, :], ACT.Copy).then_inc(p_hi, 1)
            for t in range(2):
                for q in (n + 2 * t + 2, n + 2 * t + 3):
                    if q < N_HALF:
                        hi(act, q)
                act.wait_ge(half_used, n + 2 * t + 2)
                for m in range(4):
                    o, freed = evac(act, a + t, m)
                    act.activation(sg[:, 4 * t + m, :], o, ACT.Exp, scale=-1.0).then_inc(freed, 1)
            if n + 6 < N_HALF:
                hi(act, n + 6)

        def ple_dve(dve, l, a, n):
            dve.wait_ge(p_hi, l + 1)
            dve.tensor_tensor(pL[:, :, :], pF[:, :, :], pH[:, :, :].bitcast(F32), ALU.subtract).then_inc(p_lo, 1)
            for t in range(2):
                for q in (n + 2 * t + 2, n + 2 * t + 3):
                    if q < N_HALF:
                        lo(dve, q)
                for m in range(4):
                    c = 4 * t + m
                    dve.wait_ge(acc_free[(a + t) % 2], 4 * ((a + t) // 2) + m + 1)
                    dve.tensor_scalar(sg[:, c, :], sg[:, c, :], 1.0, None, ALU.add).then_inc(ple_s, 1)
                for m in range(4):
                    c = 4 * t + m
                    dve.wait_ge(ple_s, 16 * l + 8 * t + m + 1)
                    dve.reciprocal(sg[:, c, :], sg[:, c, :]).then_inc(ple_s, 1)
            if n + 6 < N_HALF:
                lo(dve, n + 6)
            dve.wait_ge(half_used, n + 5)
            dve.wait_ge(ple_s, 16 * l + 16)
            for t in range(2):
                for m in range(4):
                    c = 4 * t + m
                    o, freed = evac(dve, a + 2 + t, m)
                    dve.tensor_tensor(sg[:, c, :], o, sg[:, c, :], ALU.mult).then_inc(freed, 1)
                for m in range(4):
                    c = 4 * t + m
                    dve.wait_ge(acc_free[(a + 2 + t) % 2], 4 * ((a + 2 + t) // 2) + m + 1)
                    dve.tensor_tensor(x[:, c, :], x[:, c, :], sg[:, c, :], ALU.add).then_inc(ple_x, 1)

        def ple_pe(pe, l, a, n, hbase):
            tile_mm(pe, a, n, hbase=hbase)
            tile_mm(pe, a + 1, n + 2)
            pe.wait_ge(p_lo, l + 1)
            pe.wait_ge(w_lo, n + 5)
            for t in range(2):
                acc_wait(pe, a + 2 + t)
                for k in range(2):
                    for m in range(4):
                        last = three(pe, bank[:, 4 * ((a + 2 + t) % 2) + m, :],
                                     wpart((n + 4) % 2, k, (4 * t + m) * P, P, D), (pH[:, k, :], pL[:, k, :]),
                                     k == 0, k == 1)
            last.then_inc(half_used, 1)

        def sp_third(sp):
            for n in range(N_MI + 2, HALF0["kv2"] + 2):
                if n == N_MO + 2:
                    sp.wait_ge(y_lo, 16 + 8)
                    sp.dma_start(pF[:, :, :], d["p"][0]).then_inc(p_in, 16)
                    for name in ("rope", "dmask"):
                        sp.dma_start(sb[name].ap(), d[name]).then_inc(par3_in, 16)
                load_half(sp, n)

        def act_third(act):
            act.wait_ge(par3_in, 32)
            act.activation(sb["gmH"][:, :, :], sb["gm"][:, :, :], ACT.Copy).then_inc(gm_hi, 1)
            stats_act(act, 5, lambda e, c: e.wait_ge(f_norm, c + 1), 47)
            apply_act(act, 5, lambda c: col("norm_a", c), None)
            for a in range(47, 55):
                n = N_MI + 2 * (a - 47)
                hi(act, n + 2)
                hi(act, n + 3)
                act.wait_ge(half_used, n + 2)
                if a < 49:
                    conv_act(act, a)
                    continue
                for m in range(4):
                    o, freed = evac(act, a, m)
                    w = slice(((a - 49) % 2) * T, ((a - 49) % 2 + 1) * T)
                    if a < 51:
                        act.activation(vM[:, m, w], o, ACT.Copy).then_inc(freed, 1)
                        if a == 49 and m == 3:
                            m_gates_act(act)
                    elif a < 53:
                        act.activation(oM[:, m, w], o, ACT.Exp, scale=-1.0).then_inc(freed, 1)
                    else:
                        q = 4 * (a - 53) + m
                        if q >= 3:
                            act.wait_ge(zz, 3 * (q - 2))
                        act.activation(tmp[:, q % 3, :], o, ACT.Exp, scale=-1.0).then_inc(zz_e, 1)
                        act.wait_ge(zz_e, q + 1)
                        act.activation(zM[:, m, w], o, ACT.Copy).then_inc(freed, 1)
                if a == 54:
                    m_rows_act(act)
            m_core_act(act)
            for a in (55, 56):
                n = N_MO + 2 * (a - 55)
                hi(act, n + 2)
                hi(act, n + 3)
            stats_act(act, 6, xw_evac(55), 57)
            apply_act(act, 6, lambda c: col("ple_norm", c), None)
            ple_act(act, 0, 57, N_G0)

        def dve_third(dve):
            dve.wait_ge(gm_hi, 1)
            dve.tensor_tensor(sb["gmL"][:, :, :], sb["gm"][:, :, :], sb["gmH"][:, :, :].bitcast(F32),
                              ALU.subtract).then_inc(gm_lo, 1)
            apply_dve(dve, 5, 5)
            dve.memset(sb["ones"][:, :], 1.0).then_inc(xc0, 1)
            dve.wait_ge(xc0, 1)
            for a in range(47, 55):
                n = N_MI + 2 * (a - 47)
                lo(dve, n + 2)
                lo(dve, n + 3)
                if a == 47:
                    dve.memset(xc[:, :, 0:3], 0.0).then_inc(xc0, 1)
                if a < 49:
                    conv_dve(dve, a)
                    continue
                if a == 49:
                    m_gates_dve(dve)
                if a < 51:
                    continue
                w = slice(((a - 49) % 2) * T, ((a - 49) % 2 + 1) * T)
                for m in range(4):
                    if a < 53:
                        q = 4 * (a - 51) + m
                        dve.wait_ge(acc_free[a % 2], 4 * (a // 2) + m + 1)
                        dve.tensor_scalar(oM[:, m, w], oM[:, m, w], 1.0, None, ALU.add).then_inc(og, 1)
                        dve.wait_ge(og, 2 * q + 1)
                        dve.reciprocal(oM[:, m, w], oM[:, m, w]).then_inc(og, 1)
                    else:
                        q = 4 * (a - 53) + m
                        e = tmp[:, q % 3, :]
                        dve.wait_ge(zz_e, q + 1)
                        dve.tensor_scalar(e, e, 1.0, None, ALU.add).then_inc(zz, 1)
                        dve.wait_ge(zz, 3 * q + 1)
                        dve.reciprocal(e, e).then_inc(zz, 1)
                        dve.wait_ge(zz, 3 * q + 2)
                        dve.wait_ge(acc_free[a % 2], 4 * (a // 2) + m + 1)
                        dve.tensor_tensor(zM[:, m, w], zM[:, m, w], e, ALU.mult).then_inc(zz, 1)
            dve.wait_ge(zz, 24)
            m_core_dve(dve)
            for a in (55, 56):
                n = N_MO + 2 * (a - 55)
                lo(dve, n + 2)
                lo(dve, n + 3)
                dve.wait_ge(half_used, n + 2)
                residual_dve(dve, a, 4 * (a - 55), None)
            apply_dve(dve, 6, 6)
            ple_dve(dve, 0, 57, N_G0)

        def pe_third(pe):
            stats_pe(pe, 5, 47)
            tile_mm(pe, 47, N_MI, hbase=40)
            for a in range(48, 55):
                if a == 50:
                    m_gates_pe(pe)
                    pe.wait_ge(r_act, 2)
                tile_mm(pe, a, N_MI + 2 * (a - 47), tok=a >= 49)
            pe.wait_ge(acc_free[0], 4 * 28)
            m_rows_pe(pe)
            m_core_pe(pe)
            pe.wait_ge(y_lo, 16 + 8)
            for a in (55, 56):
                tile_mm(pe, a, N_MO + 2 * (a - 55))
            stats_pe(pe, 6, 57)
            ple_pe(pe, 0, 57, N_G0, 48)

        N_K2, N_DI, N_DO, N_G1 = (HALF0[n] for n in ("kv2", "d_in", "d_out", "ple1g"))
        rp, hn_cp, hn_sq, hn_mm, hn_ex, hn_y = (sem(n) for n in (
            "rp", "hn_cp", "hn_sq", "hn_mm", "hn_ex", "hn_y"))
        v_moved, zd, zd_e = sem("v_moved"), sem("zd"), sem("zd_e")
        d_mm, d_max, d_exp, d_t, d_pt, d_o, d_ev = (sem(n) for n in (
            "d_mm", "d_max", "d_exp", "d_t", "d_pt", "d_o", "d_ev"))
        k_t, k_ev, k_w, k_e, k_b, k_bx, k_y = (sem(n) for n in (
            "k_t", "k_ev", "k_w", "k_e", "k_b", "k_bx", "k_y"))
        qD, kD, vD, vC, zD, rw, sw, hq, hr = (sb[n] for n in ("qD", "kD", "vD", "vC", "zD", "rw", "sw", "hq", "hr"))
        sD, pD, ptD, dmask, nmR, nmS, rsR, zR = (sb[n] for n in ("sD", "pD", "ptD", "dmask", "nmR", "nmS", "rsR", "zR"))
        D_H = 4
        HTILES = [61, 63, 64, 65]

        def head_copy(act, t):
            a = HTILES[t]
            for m in range(4):
                e = 4 * t + m
                o = bank[:, 4 * (a % 2) + m, :]
                if t >= 1:
                    act.wait_ge(hn_y, 4 * (e - 4) + 4)
                act.activation(rw[:, m, :], o, ACT.Copy).then_inc(hn_cp, 1)
                act.activation(sw[0:HD, m, :], o[HD:P, :], ACT.Copy).then_inc(hn_cp, 1)
                act.activation(sw[HD:P, m, :], o[0:HD, :], ACT.Copy).then_inc(hn_cp, 1)

        def head_stat(act, t):
            a = HTILES[t]
            for m in range(4):
                e = 4 * t + m
                if e >= 2:
                    act.wait_ge(hn_mm, e - 1)
                act.wait_ge(hn_cp, 3 * e + 3)
                act.activation(hq[:, e % 2, :], rw[:, m, :], ACT.Square).then_inc(hn_sq, 1)
                if m >= 1:
                    head_rstd(act, a, e - 1)
            head_rstd(act, a, 4 * t + 3)

        def head_rstd(act, a, e):
            act.wait_ge(hn_mm, e + 1)
            if e >= 2:
                act.wait_ge(hn_y, 4 * (e - 2) + 4)
            act.activation(hr[:, e % 2, :], bank[:, 4 * (a % 2) + e % 4, :], ACT.Ln, bias=one[:, 1:2],
                           scale=float(D // P)).then_inc(acc_free[a % 2], 1)
            act.wait_ge(acc_free[a % 2], 4 * (a // 2) + e % 4 + 1)
            act.activation(hr[:, e % 2, :], hr[:, e % 2, :], ACT.Exp, scale=-0.5).then_inc(hn_ex, 1)

        def head_pe(pe, t):
            a = HTILES[t]
            for m in range(4):
                e = 4 * t + m
                pe.wait_ge(hn_sq, e + 1)
                pe.matmul(bank[:, 4 * (a % 2) + m, :], sb["mean"][:, :], hq[:, e % 2, :], start=True, stop=True)\
                    .then_inc(hn_mm, 1)

        def head_dve(dve, t):
            tab = sb["rpK"] if t == 0 else sb["rpQ"]
            for m in range(4):
                e = 4 * t + m
                dst = kD[:, m, :] if t == 0 else qD[:, 4 * (t - 1) + m, :]
                dve.wait_ge(hn_sq, e + 1)
                dve.wait_ge(hn_cp, 3 * e + 3)
                dve.tensor_tensor(rw[:, m, :], rw[:, m, :], tab[:, 0, :], ALU.mult).then_inc(hn_y, 1)
                dve.tensor_tensor(sw[:, m, :], sw[:, m, :], tab[:, 1, :], ALU.mult).then_inc(hn_y, 1)
                dve.wait_ge(hn_y, 4 * e + 2)
                dve.tensor_tensor(rw[:, m, :], rw[:, m, :], sw[:, m, :], ALU.add).then_inc(hn_y, 1)
                dve.wait_ge(hn_y, 4 * e + 3)
                dve.wait_ge(hn_ex, e + 1)
                dve.tensor_tensor(dst, rw[:, m, :], hr[:, e % 2, :], ALU.mult).then_inc(hn_y, 1)

        DU = 48

        def d_unit(u):
            c, n = divmod(u, 4)
            g, h = divmod(c, 4)
            w = 256 if g == 0 and n > 0 else P
            return c, n, g, h, w

        def stat_col(u):
            c, n, g, h, w = d_unit(u)
            return 16 * g + 4 * n + h

        def d_pe(pe):
            pe.wait_ge(hn_y, 64)
            pe.wait_ge(acc_free[1], 4 * 33)
            pe.wait_ge(acc_free[0], 4 * 34)
            pe.wait_ge(v_moved, 32)

            def scores(u):
                c, n, g, h, w = d_unit(u)
                if u >= 2:
                    pe.wait_ge(d_max, u - 1)
                if g == 0:
                    q, k = qD[:, c, n * P:(n + 1) * P], kD[:, h, (n + 1) * P - w:(n + 1) * P]
                else:
                    q, k = (z.rearrange("p (u r) -> p r u", r=4)[:, n, :] for z in (qD[:, c, :], kD[:, h, :]))
                pe.matmul(bank[:, u % 2, 0:w], q, k, start=True, stop=True).then_inc(d_mm, 1)

            def turn(u):
                w = d_unit(u)[4]
                pe.wait_ge(d_exp, u + 1)
                if u >= 2:
                    pe.wait_ge(d_pt, u - 1)
                for j in range(w // P):
                    last = pe.transpose(bank[:, 2 + u % 2, j * P:(j + 1) * P], pD[:, u % 2, j * P:(j + 1) * P],
                                        ident[:, :])
                last.then_inc(d_t, 1)

            def values(u):
                c, n, g, h, w = d_unit(u)
                pe.wait_ge(d_pt, u + 1)
                if n == 0 and c >= 2:
                    pe.wait_ge(d_ev, c - 1)
                k = w // P
                for j in range(k):
                    v = vD[:, n - (k - 1) + j, h * P:(h + 1) * P] if g == 0 else vC[:, n, h * P:(h + 1) * P]
                    last = pe.matmul(bank[:, 4 + c % 2, n * P:(n + 1) * P], v, ptD[:, u % 2, j * P:(j + 1) * P],
                                     start=j == 0, stop=j == k - 1)
                last.then_inc(d_o, 1)

            for u in range(-1, DU + 1):
                if u + 1 < DU:
                    scores(u + 1)
                if 0 <= u - 1:
                    values(u - 1)
                if 0 <= u < DU:
                    turn(u)
            for s, src in enumerate((nm, rs)):
                for g in range(3):
                    for n in range(4):
                        last = pe.transpose(bank[0:4, (0, 1, 2, 3, 6, 7)[3 * s + g],
                                            n * P:(n + 1) * P], src[:, 16 * g + 4 * n:16 * g + 4 * n + 4], ident[:, :])
                    last.then_inc(k_t, 1)
            for h in range(D_H):
                for g in range(3):
                    b = 3 * h + g
                    if b >= 3:
                        pe.wait_ge(k_bx, b - 2)
                    if b == 0:
                        pe.wait_ge(k_w, 14)
                    pe.matmul(bank[:, b % 3, :], ident[0:4, h:h + 1].to_broadcast([4, P]), nmR[:, g, :],
                              start=True, stop=True).then_inc(k_b, 1)

        def d_dve(dve):
            def mask_max(u):
                c, n, g, h, w = d_unit(u)
                dve.wait_ge(d_mm, u + 1)
                if u >= 2:
                    dve.wait_ge(d_exp, u - 1)
                m = dmask[:, 256 - w:256] if g == 0 else dmask[:, (g + 1) * P:(g + 2) * P]
                s = stat_col(u)
                dve.tensor_tensor_reduce(sD[:, u % 2, 0:w], bank[:, u % 2, 0:w], m, -MK, BIG, ALU.add, ALU.min,
                                         nm[:, s:s + 1]).then_inc(d_max, 1)

            def copy_out(u):
                w = d_unit(u)[4]
                dve.wait_ge(d_t, u + 1)
                if u >= 2:
                    dve.wait_ge(d_o, u - 1)
                dve.tensor_copy(ptD[:, u % 2, 0:w], bank[:, 2 + u % 2, 0:w]).then_inc(d_pt, 1)

            mask_max(0)
            for u in range(DU):
                if u + 1 < DU:
                    mask_max(u + 1)
                copy_out(u)
            dve.wait_ge(k_ev, 6)
            q = [nmR[:, g, :] for g in range(3)]
            r = [rsR[:, g, :] for g in range(3)]
            m, z = nmS[:, :], zR[:, :]
            ops = [
                (m, q[0], q[1], ALU.min), (m, m, q[2], ALU.min),
                (q[0], m, q[0], ALU.subtract), (q[1], m, q[1], ALU.subtract), (q[2], m, q[2], ALU.subtract),
            ]
            n = 0
            for o, a, b, op in ops:
                dve.tensor_tensor(o, a, b, op).then_inc(k_w, 1)
                n += 1
                dve.wait_ge(k_w, n)
            dve.wait_ge(k_e, 1)
            for o, a, b, op in [(r[0], r[0], q[0], ALU.mult), (r[1], r[1], q[1], ALU.mult), (r[2], r[2], q[2], ALU.mult),
                                (z, r[0], r[1], ALU.add), (z, z, r[2], ALU.add)]:
                dve.tensor_tensor(o, a, b, op).then_inc(k_w, 1)
                n += 1
                dve.wait_ge(k_w, n)
            dve.reciprocal(z, z).then_inc(k_w, 1)
            dve.wait_ge(k_w, n + 1)
            for g in range(3):
                dve.tensor_tensor(q[g], q[g], z, ALU.mult).then_inc(k_w, 1)
            for h in range(D_H):
                for g in range(3):
                    b = 3 * h + g
                    dve.wait_ge(k_b, b + 1)
                    if b == 0:
                        dve.wait_ge(d_ev, 12)
                    o = qD[:, 4 * g + h, :]
                    dve.tensor_tensor(o, o, bank[:, b % 3, :], ALU.mult).then_inc(k_bx, 1)
                dve.wait_ge(k_bx, 3 * h + 3)
                y = qD[:, h, :]
                for n, (a, op) in enumerate(((qD[:, 4 + h, :], ALU.add), (qD[:, 8 + h, :], ALU.add),
                                             (zD[:, h, :], ALU.mult))):
                    dve.tensor_tensor(y, y, a, op).then_inc(k_y, 1)
                    dve.wait_ge(k_y, 3 * h + n + 1)
                dve.wait_ge(y_hi, 24 + h + 1)
                dve.tensor_tensor(hL[:, h, :], y, hH[:, h, :].bitcast(F32), ALU.subtract).then_inc(y_lo, 1)

        def d_act(act):
            def exps(u):
                c, n, g, h, w = d_unit(u)
                act.wait_ge(d_max, u + 1)
                if u >= 2:
                    act.wait_ge(d_t, u - 1)
                s = stat_col(u)
                act.activation(pD[:, u % 2, 0:w], sD[:, u % 2, 0:w], ACT.Exp, bias=nm[:, s:s + 1], scale=-1.0,
                               accum_out=rs[:, s:s + 1]).then_inc(d_exp, 1)

            exps(0)
            for u in range(DU + 2):
                if u + 1 < DU:
                    exps(u + 1)
                c = (u - 1) // 4
                if u - 1 >= 0 and (u - 1) % 4 == 3 and c < 12:
                    act.wait_ge(d_o, 4 * c + 4)
                    o = bank[:, 4 + c % 2, :]
                    if c < 4:
                        act.activation(qD[:, c, :], o, ACT.Copy).then_inc(d_ev, 1)
                    else:
                        act.activation(qD[:, c, :].rearrange("p (u r) -> p r u", r=4),
                                       o.rearrange("p (r u) -> p r u", r=4), ACT.Copy).then_inc(d_ev, 1)
            for s, dst in enumerate((nmR, rsR)):
                for g in range(3):
                    act.wait_ge(k_t, 3 * s + g + 1)
                    o = bank[0:4, (0, 1, 2, 3, 6, 7)[3 * s + g], :]
                    if g == 0:
                        act.activation(dst[:, g, :], o, ACT.Copy).then_inc(k_ev, 1)
                    else:
                        act.activation(dst[:, g, :].rearrange("p (u r) -> p r u", r=4),
                                       o.rearrange("p (r u) -> p r u", r=4), ACT.Copy).then_inc(k_ev, 1)
            act.wait_ge(k_w, 5)
            act.activation(nmR[:, :, :], nmR[:, :, :], ACT.Exp).then_inc(k_e, 1)
            for h in range(D_H):
                act.wait_ge(k_y, 3 * h + 3)
                act.activation(hH[:, h, :], qD[:, h, :], ACT.Copy).then_inc(y_hi, 1)

        def sp_fourth(sp):
            vscr = nc.dram_tensor("values_by_token", (T, T), F32, kind="Internal").ap()
            for n in range(N_K2 + 2, N_HALF):
                if n == N_K2 + 6:
                    sp.wait_ge(acc_free[0], 4 * 32)
                    sp.dma_start(vscr.rearrange("(i p) d -> p i d", p=P), vD[:, :, :]).then_inc(v_moved, 16)
                    sp.wait_ge(v_moved, 16)
                    sp.dma_start(vC[:, :, :], vscr.rearrange("(u r) d -> u r d", r=4)).then_inc(v_moved, 16)
                if n == N_DO + 2:
                    sp.wait_ge(y_lo, 24 + 4)
                    sp.dma_start(pF[:, :, :], d["p"][1]).then_inc(p_in, 16)
                load_half(sp, n)
            sp.wait_ge(ple_x, 16)
            sp.dma_start(out, x[:, :, :]).then_inc(out_done, 16)
            sp.wait_ge(out_done, 16)

        def act_fourth(act):
            def split2(a, n):
                hi(act, n + 2)
                hi(act, n + 3)
                act.wait_ge(half_used, n + 2)

            stats_act(act, 7, lambda e, c: e.wait_ge(ple_x, c + 1), 61)
            apply_act(act, 7, lambda c: col("norm_kv", c), None)
            split2(61, N_K2)
            head_copy(act, 0)
            split2(62, N_K2 + 2)
            head_stat(act, 0)
            for m in range(4):
                o, freed = evac(act, 62, m)
                act.activation(vD[:, m, :], o, ACT.Copy).then_inc(freed, 1)
            apply_act(act, 8, lambda c: col("norm_b", c), None)
            split2(63, N_DI)
            head_copy(act, 1)
            split2(64, N_DI + 2)
            head_stat(act, 1)
            head_copy(act, 2)
            split2(65, N_DI + 4)
            head_stat(act, 2)
            head_copy(act, 3)
            split2(66, N_DI + 6)
            head_stat(act, 3)
            for m in range(4):
                o, freed = evac(act, 66, m)
                if m >= 2:
                    act.wait_ge(zd, 3 * (m - 1))
                act.activation(sb["hz"][:, m % 2, :], o, ACT.Exp, scale=-1.0).then_inc(zd_e, 1)
                act.wait_ge(zd_e, m + 1)
                act.activation(zD[:, m, :], o, ACT.Copy).then_inc(freed, 1)
            d_act(act)
            hi(act, N_DO + 2)
            hi(act, N_DO + 3)
            stats_act(act, 8, xw_evac(67), 69)
            apply_act(act, 9, lambda c: col("ple_norm", 8 + c), None)
            ple_act(act, 1, 69, N_G1)

        def dve_fourth(dve):
            dve.wait_ge(par3_in, 64)
            for tab, g in (("rpK", "knorm"), ("rpQ", "qnorm")):
                for j in range(2):
                    dve.tensor_scalar(sb[tab][:, j, :], sb["rope"][:, j, :], col(g + "_s" * j), None, ALU.mult)\
                        .then_inc(rp, 1)
            apply_dve(dve, 7, 7)
            dve.wait_ge(rp, 4)
            lo(dve, N_K2 + 2)
            lo(dve, N_K2 + 3)
            lo(dve, N_K2 + 4)
            lo(dve, N_K2 + 5)
            head_dve(dve, 0)
            apply_dve(dve, 8, 7)
            for t in range(1, 4):
                lo(dve, N_DI + 2 * t)
                lo(dve, N_DI + 2 * t + 1)
                if t >= 2:
                    head_dve(dve, t - 1)
            lo(dve, N_DI + 8)
            lo(dve, N_DI + 9)
            head_dve(dve, 3)
            for m in range(4):
                z = sb["hz"][:, m % 2, :]
                dve.wait_ge(zd_e, m + 1)
                dve.tensor_scalar(z, z, 1.0, None, ALU.add).then_inc(zd, 1)
                dve.wait_ge(zd, 3 * m + 1)
                dve.reciprocal(z, z).then_inc(zd, 1)
                dve.wait_ge(zd, 3 * m + 2)
                dve.wait_ge(acc_free[0], 4 * 33 + m + 1)
                dve.tensor_tensor(zD[:, m, :], zD[:, m, :], z, ALU.mult).then_inc(zd, 1)
            dve.wait_ge(zd, 12)
            d_dve(dve)
            lo(dve, N_DO + 2)
            lo(dve, N_DO + 3)
            for a in (67, 68):
                dve.wait_ge(half_used, N_DO + a - 66)
                residual_dve(dve, a, 4 * (a - 67), None)
            apply_dve(dve, 9, 8)
            ple_dve(dve, 1, 69, N_G1)

        def pe_fourth(pe):
            stats_pe(pe, 7, 61)
            tile_mm(pe, 61, N_K2, hbase=56)
            tile_mm(pe, 62, N_K2 + 2, tok=True)
            head_pe(pe, 0)
            tile_mm(pe, 63, N_DI, hbase=64)
            tile_mm(pe, 64, N_DI + 2)
            head_pe(pe, 1)
            tile_mm(pe, 65, N_DI + 4)
            head_pe(pe, 2)
            tile_mm(pe, 66, N_DI + 6)
            head_pe(pe, 3)
            d_pe(pe)
            pe.wait_ge(y_lo, 24 + 4)
            for a in (67, 68):
                n = N_DO + a - 67
                acc_wait(pe, a)
                pe.wait_ge(w_lo, n + 1)
                for k in range(4):
                    for m in range(4):
                        last = three(pe, bank[:, 4 * (a % 2) + m, :], wpart(n % 2, k, m * P, P),
                                     (hH[:, k, :], hL[:, k, :]), k == 0, k == 3)
                last.then_inc(half_used, 1)
            stats_pe(pe, 8, 69)
            ple_pe(pe, 1, 69, N_G1, 72)

        @block.sync
        def _(sp):
            sp_first(sp)
            mlp_sp(sp, 0)
            sp_second(sp)
            sp_third(sp)
            sp_fourth(sp)

        @block.scalar
        def _(act):
            act.preload_act_table_set("natural_log_exp_and_others")
            act_first(act)
            act_second(act)
            act_third(act)
            act_fourth(act)

        @block.vector
        def _(dve):
            dve_first(dve)
            dve_second(dve)
            dve_third(dve)
            dve_fourth(dve)

        @block.tensor
        def _(pe):
            pe_first(pe)
            pe_second(pe)
            pe_third(pe)
            pe_fourth(pe)


def kernel(**inputs):
    import concourse.bacc as _bacc
    from concourse.bass_utils import run_bass_kernel_spmd as _run

    arrays = lay_out(inputs)
    nc = _bacc.Bacc("TRN2", target_bir_lowering=False, num_devices=1)
    d = {k: nc.dram_tensor(k + "_d", a.shape, F32, kind="ExternalInput").ap() for k, a in arrays.items()}
    out = nc.dram_tensor("out_d", (P, KC, T), F32, kind="ExternalOutput").ap()
    program(nc, d, out)
    r = _run(nc, [{k + "_d": a for k, a in arrays.items()}], core_ids=[0])
    y = r.results[0]["out_d"]
    return np.ascontiguousarray(y.transpose(2, 1, 0).reshape(1, T, D))
```
